# Optimizing a Trainium2 kernel written in Bass

```python
import math
import jax, jax.numpy as jnp
from jax import lax
import numpy as np

D_MODEL = 1024
BATCH = 1
SEQ = 512
DEPTH = 1

DA_HEADS = 8
DA_DH = 64
DA_QK = DA_HEADS * 2 * DA_DH
DA_V = DA_HEADS * 2 * DA_DH
DA_QBLOCK = 128
ROPE_THETA = 10000.0

GDN_HEADS = 8
GDN_DK = 128
GDN_DV = 128
GDN_QK = GDN_HEADS * GDN_DK
GDN_VW = GDN_HEADS * GDN_DV
GDN_CONV_DIM = 2 * GDN_QK + GDN_VW
CONV_K = 5
GDN_CHUNK = 64

N_EXPERTS = 16
EXPERT_FF = 2048
CAP_FACTOR = 2

NORM_EPS = 1e-6
IN_WIDTH = 2 * DA_QK + DA_V + GDN_CONV_DIM + GDN_VW + 4 * GDN_HEADS + 2 * D_MODEL


def rmsnorm(t, w, eps=NORM_EPS):
    t32 = t.astype(jnp.float32)
    y = t32 * lax.rsqrt(jnp.mean(t32 * t32, axis=-1, keepdims=True) + eps)
    return (y * w.astype(jnp.float32)).astype(t.dtype)

def l2norm(t, eps=1e-6):
    t32 = t.astype(jnp.float32)
    return t32 * lax.rsqrt(jnp.sum(t32 * t32, axis=-1, keepdims=True) + eps)

def rope_tables(seq, dim):
    inv = ROPE_THETA ** (-jnp.arange(0, dim, 2, dtype=jnp.float32) / dim)
    ang = jnp.arange(seq, dtype=jnp.float32)[:, None] * inv[None, :]
    ang = jnp.concatenate([ang, ang], axis=-1)
    return jnp.cos(ang), jnp.sin(ang)

def apply_rope(t, cos, sin):
    half = t.shape[-1] // 2
    t32 = t.astype(jnp.float32)
    rot = jnp.concatenate([-t32[..., half:], t32[..., :half]], axis=-1)
    shp = (1, t.shape[1]) + (1,) * (t.ndim - 3) + (t.shape[-1],)
    return (t32 * cos.reshape(shp) + rot * sin.reshape(shp)).astype(t.dtype)

def diff_attention(q, k, v, lam):
    b, s, h, _, dh = q.shape
    nb = s // DA_QBLOCK
    scale = dh ** -0.5
    qb = jnp.moveaxis(q.reshape(b, nb, DA_QBLOCK, h, 2, dh), 1, 0)

    def block(qblk):
        sc = jnp.einsum('bqhtd,bkhtd->bhtqk', qblk, k).astype(jnp.float32) * scale
        pr = jax.nn.softmax(sc, axis=-1)
        pd = pr[:, :, 0] - lam * pr[:, :, 1]
        return jnp.einsum('bhqk,bkhe->bqhe', pd.astype(v.dtype), v)

    o = lax.map(block, qb)
    return jnp.moveaxis(o, 0, 1).reshape(b, s, h, v.shape[-1])

def gated_delta_rule_chunked(q, k, v, g, beta):
    b, s, h, dk = q.shape
    dv = v.shape[-1]
    n = s // GDN_CHUNK

    def chunks(t):
        t = t.astype(jnp.float32).reshape((b, n, GDN_CHUNK, h) + t.shape[3:])
        return jnp.moveaxis(t, 3, 1)

    q = chunks(q) * dk ** -0.5
    k = chunks(k)
    v = chunks(v)
    g = jnp.cumsum(chunks(g), axis=-1)
    beta = chunks(beta)

    incl = jnp.tril(jnp.ones((GDN_CHUNK, GDN_CHUNK), dtype=bool))
    strict = jnp.tril(jnp.ones((GDN_CHUNK, GDN_CHUNK), dtype=bool), k=-1)
    gdiff = g[..., :, None] - g[..., None, :]
    decay = jnp.where(incl, jnp.exp(jnp.where(incl, gdiff, 0.0)), 0.0)

    k_beta = k * beta[..., None]
    a_mat = jnp.where(strict, jnp.einsum('bhnid,bhnjd->bhnij', k_beta, k) * decay, 0.0)
    t_mat = a_mat + jnp.eye(GDN_CHUNK, dtype=jnp.float32)
    rhs = jnp.concatenate([v * beta[..., None], k_beta * jnp.exp(g)[..., None]], axis=-1)
    sol = lax.linalg.triangular_solve(t_mat, rhs, left_side=True, lower=True,
                                      unit_diagonal=True)
    u, w = sol[..., :dv], sol[..., dv:]

    qk = jnp.where(incl, jnp.einsum('bhnid,bhnjd->bhnij', q, k) * decay, 0.0)
    q_dec = q * jnp.exp(g)[..., None]
    k_dec = k * jnp.exp(g[..., -1:] - g)[..., None]
    g_last = jnp.exp(g[..., -1])

    def step(state, inp):
        qk_c, qd_c, kd_c, u_c, w_c, gl_c = inp
        v_new = u_c - jnp.einsum('bhcd,bhde->bhce', w_c, state)
        o_c = (jnp.einsum('bhcd,bhde->bhce', qd_c, state)
               + jnp.einsum('bhij,bhje->bhie', qk_c, v_new))
        state = state * gl_c[..., None, None] + jnp.einsum('bhcd,bhce->bhde', kd_c, v_new)
        return state, o_c

    xs = tuple(jnp.moveaxis(t, 2, 0) for t in (qk, q_dec, k_dec, u, w, g_last))
    state0 = jnp.zeros((b, h, dk, dv), jnp.float32)
    _, o = lax.scan(step, state0, xs)
    o = jnp.moveaxis(o, 0, 2)
    return jnp.moveaxis(o, 1, 3).reshape(b, s, h, dv)

def centred_depthwise_conv(t, w):
    c = t.shape[-1]
    pad = CONV_K // 2
    return lax.conv_general_dilated(
        t, w[:, None, :].astype(t.dtype), window_strides=(1,), padding=[(pad, pad)],
        dimension_numbers=('NWC', 'WIO', 'NWC'), feature_group_count=c)

def expert_choice_ffn(h, w_router, w_gate, w_up, w_down):
    b, s, d = h.shape
    cap = CAP_FACTOR * s // N_EXPERTS
    logits = jnp.einsum('bsd,de->bse', h, w_router).astype(jnp.float32)
    aff = jax.nn.softmax(logits, axis=-1)
    top_val, top_idx = lax.top_k(jnp.swapaxes(aff, 1, 2), cap)
    xs = jax.vmap(lambda hb, ib: hb[ib])(h, top_idx)
    gt = jnp.einsum('becd,edf->becf', xs, w_gate)
    up = jnp.einsum('becd,edf->becf', xs, w_up)
    ye = jnp.einsum('becf,efd->becd', jax.nn.silu(gt) * up, w_down)
    ye = ye * top_val[..., None].astype(ye.dtype)

    def scatter(yb, ib):
        return jnp.zeros((s, d), yb.dtype).at[ib.reshape(-1)].add(yb.reshape(-1, d))

    return jax.vmap(scatter)(ye, top_idx)

def first_inputs(seed: int = 0) -> dict:
    key = jax.random.key(seed)
    ks = jax.random.split(key, 32)
    f32 = jnp.float32

    def nrm(k, shape, scale):
        return jax.random.normal(k, shape, f32) * scale

    def gain(k, n):
        return 1.0 + 0.02 * jax.random.normal(k, (DEPTH, n), f32)

    def a_log(k):
        return jnp.log(jax.random.uniform(k, (DEPTH, GDN_HEADS), f32, 1.0, 16.0))

    def dt_bias(k):
        dt = jnp.exp(jax.random.uniform(k, (DEPTH, GDN_HEADS), f32,
                                        math.log(1e-3), math.log(1e-1)))
        return dt + jnp.log(-jnp.expm1(-dt))

    return {
        "x": nrm(ks[0], (BATCH, SEQ, D_MODEL), 1.0),
        "norm1_w": gain(ks[1], D_MODEL),
        "w_in": nrm(ks[2], (DEPTH, D_MODEL, IN_WIDTH), D_MODEL ** -0.5),
        "conv_w": nrm(ks[3], (DEPTH, CONV_K, GDN_CONV_DIM), CONV_K ** -0.5),
        "a_log_fwd": a_log(ks[4]),
        "dt_bias_fwd": dt_bias(ks[5]),
        "a_log_bwd": a_log(ks[6]),
        "dt_bias_bwd": dt_bias(ks[7]),
        "gdn_norm_w": gain(ks[8], GDN_DV),
        "lambda_q1": nrm(ks[9], (DEPTH, DA_DH), 0.1),
        "lambda_k1": nrm(ks[10], (DEPTH, DA_DH), 0.1),
        "lambda_q2": nrm(ks[11], (DEPTH, DA_DH), 0.1),
        "lambda_k2": nrm(ks[12], (DEPTH, DA_DH), 0.1),
        "subln_w": gain(ks[13], 2 * DA_DH),
        "w_proj_attn": nrm(ks[14], (DEPTH, DA_V, D_MODEL), DA_V ** -0.5),
        "w_proj_gdn": nrm(ks[15], (DEPTH, GDN_VW, D_MODEL), GDN_VW ** -0.5),
        "w_out": nrm(ks[16], (DEPTH, D_MODEL, D_MODEL), D_MODEL ** -0.5),
        "norm2_w": gain(ks[17], D_MODEL),
        "w_router": nrm(ks[18], (DEPTH, D_MODEL, N_EXPERTS), D_MODEL ** -0.5),
        "w_gate": nrm(ks[19], (DEPTH, N_EXPERTS, D_MODEL, EXPERT_FF), D_MODEL ** -0.5),
        "w_up": nrm(ks[20], (DEPTH, N_EXPERTS, D_MODEL, EXPERT_FF), D_MODEL ** -0.5),
        "w_down": nrm(ks[21], (DEPTH, N_EXPERTS, EXPERT_FF, D_MODEL), EXPERT_FF ** -0.5),
        "norm_f_w": 1.0 + 0.02 * jax.random.normal(ks[22], (D_MODEL,), f32),
    }

def first_block(x, norm1_w, w_in, conv_w, a_log_fwd, dt_bias_fwd, a_log_bwd, dt_bias_bwd,
              gdn_norm_w, lambda_q1, lambda_k1, lambda_q2, lambda_k2, subln_w,
              w_proj_attn, w_proj_gdn, w_out, norm2_w, w_router, w_gate, w_up, w_down,
              norm_f_w):
    b, s, _ = x.shape
    cos, sin = rope_tables(s, DA_DH)
    sizes = [DA_QK, DA_QK, DA_V, GDN_CONV_DIM, GDN_VW,
             GDN_HEADS, GDN_HEADS, GDN_HEADS, GDN_HEADS, D_MODEL, D_MODEL]
    split_at = [int(v) for v in np.cumsum(sizes)[:-1]]

    for l in range(DEPTH):
        lambda_init = 0.8 - 0.6 * math.exp(-0.3 * l)
        h = rmsnorm(x, norm1_w[l])
        p = jnp.einsum('bsd,dn->bsn', h, w_in[l])
        (qa, ka, va, qkv_g, z, a_f, a_b, b_f, b_b, gate_a, gate_g) = jnp.split(p, split_at, axis=-1)

        qa = apply_rope(qa.reshape(b, s, DA_HEADS, 2, DA_DH), cos, sin)
        ka = apply_rope(ka.reshape(b, s, DA_HEADS, 2, DA_DH), cos, sin)
        va = va.reshape(b, s, DA_HEADS, 2 * DA_DH)
        lam = (jnp.exp(jnp.sum(lambda_q1[l].astype(jnp.float32) * lambda_k1[l].astype(jnp.float32)))
               - jnp.exp(jnp.sum(lambda_q2[l].astype(jnp.float32) * lambda_k2[l].astype(jnp.float32)))
               + lambda_init)
        oa = diff_attention(qa, ka, va, lam)
        oa = rmsnorm(oa, subln_w[l]) * (1.0 - lambda_init)
        ya = jnp.einsum('bse,ed->bsd', oa.reshape(b, s, DA_V).astype(x.dtype), w_proj_attn[l])

        qkv_g = jax.nn.silu(centred_depthwise_conv(qkv_g, conv_w[l]))
        qg, kg, vg = jnp.split(qkv_g, [GDN_QK, 2 * GDN_QK], axis=-1)
        qg = l2norm(qg.reshape(b, s, GDN_HEADS, GDN_DK))
        kg = l2norm(kg.reshape(b, s, GDN_HEADS, GDN_DK))
        vg = vg.reshape(b, s, GDN_HEADS, GDN_DV).astype(jnp.float32)
        g_f = -jnp.exp(a_log_fwd[l].astype(jnp.float32)) * jax.nn.softplus(
            (a_f + dt_bias_fwd[l]).astype(jnp.float32))
        g_b = -jnp.exp(a_log_bwd[l].astype(jnp.float32)) * jax.nn.softplus(
            (a_b + dt_bias_bwd[l]).astype(jnp.float32))
        beta_f = jax.nn.sigmoid(b_f.astype(jnp.float32))
        beta_b = jax.nn.sigmoid(b_b.astype(jnp.float32))
        o_fwd = gated_delta_rule_chunked(qg, kg, vg, g_f, beta_f)
        flip = lambda t: jnp.flip(t, axis=1)
        o_bwd = flip(gated_delta_rule_chunked(flip(qg), flip(kg), flip(vg), flip(g_b), flip(beta_b)))
        og = rmsnorm(o_fwd + o_bwd, gdn_norm_w[l])
        og = og * jax.nn.silu(z.reshape(b, s, GDN_HEADS, GDN_DV).astype(jnp.float32))
        yg = jnp.einsum('bse,ed->bsd', og.reshape(b, s, GDN_VW).astype(x.dtype), w_proj_gdn[l])

        merged = jax.nn.sigmoid(gate_a) * ya + jax.nn.sigmoid(gate_g) * yg
        x = x + jnp.einsum('bsd,de->bse', merged, w_out[l])

        h2 = rmsnorm(x, norm2_w[l])
        x = x + expert_choice_ffn(h2, w_router[l], w_gate[l], w_up[l], w_down[l])

    return rmsnorm(x, norm_f_w)


CHUNK = 64
BAND_PREV = 8
BAND = (BAND_PREV + 1) * CHUNK
REL_CLIP = 256
N_REL = REL_CLIP + CHUNK

W_A = D_MODEL // 2
HEAD_A = 64
H_A = W_A // HEAD_A
W_B = D_MODEL // 2
HEAD_B = 64
H_B = W_B // HEAD_B
DECAY_LORA = 64
A_LORA = 64
GATE_LORA = 128
D_FF = 4 * D_MODEL

ATT_COLS = 3 * W_A
RWKV_COLS = 3 * W_B + DECAY_LORA + A_LORA + GATE_LORA
GATE_COLS = 2 * D_MODEL
IN_COLS = ATT_COLS + RWKV_COLS + GATE_COLS

RMS_EPS = 1e-6
GN_EPS = HEAD_B * 1e-5
NEG_INF = -1e30


def rms_norm(x, g):
    xf = x.astype(jnp.float32)
    y = xf * lax.rsqrt(jnp.mean(xf * xf, axis=-1, keepdims=True) + RMS_EPS)
    return (y * g.astype(jnp.float32)).astype(x.dtype)

def chunk_band_attention(q, k, v, rel_bias):
    b, s, h, d = q.shape
    nc = s // CHUNK
    qc = q.reshape(b, nc, CHUNK, h, d)
    pad = ((0, 0), (BAND_PREV * CHUNK, 0), (0, 0), (0, 0))
    kp = jnp.pad(k, pad).reshape(b, nc + BAND_PREV, CHUNK, h, d)
    vp = jnp.pad(v, pad).reshape(b, nc + BAND_PREV, CHUNK, h, d)
    kb = jnp.concatenate([kp[:, o:o + nc] for o in range(BAND_PREV + 1)], axis=2)
    vb = jnp.concatenate([vp[:, o:o + nc] for o in range(BAND_PREV + 1)], axis=2)
    scores = jnp.einsum('bnqhd,bnkhd->bnhqk', qc, kb).astype(jnp.float32) * (d ** -0.5)
    qi = jnp.arange(CHUNK)[:, None]
    kj = jnp.arange(BAND)[None, :]
    dist = qi + BAND_PREV * CHUNK - kj
    idx = jnp.clip(dist, -(CHUNK - 1), REL_CLIP) + (CHUNK - 1)
    bias = rel_bias.astype(jnp.float32)[:, idx]
    valid = (jnp.arange(nc)[:, None] - BAND_PREV + kj // CHUNK) >= 0
    scores = jnp.where(valid[None, :, None, None, :], scores + bias[None, None], NEG_INF)
    p = jax.nn.softmax(scores, axis=-1)
    out = jnp.einsum('bnhqk,bnkhd->bnqhd', p.astype(vb.dtype), vb)
    return out.reshape(b, s, h * d)

def rwkv7_time_mix(p, shift_mu, w0, w2, a0, a2, g2, k_k, k_a, r_k, ln_x_w, ln_x_b):
    b, s, _ = p.shape
    prev = jnp.pad(p, ((0, 0), (1, 0), (0, 0)))[:, :-1]
    p = p + (prev - p) * shift_mu
    splits = [W_B, 2 * W_B, 3 * W_B, 3 * W_B + DECAY_LORA, 3 * W_B + DECAY_LORA + A_LORA]
    r, k, v, cw, ca, cg = jnp.split(p, splits, axis=-1)
    w_log = -jax.nn.softplus(-(w0 + jnp.tanh(cw) @ w2)) - 0.5
    decay = jnp.exp(-jnp.exp(w_log.astype(jnp.float32)))
    a = jax.nn.sigmoid(a0 + ca @ a2)
    g = jax.nn.sigmoid(cg) @ g2

    def heads(t):
        return t.reshape(b, s, H_B, HEAD_B).astype(jnp.float32)

    kk = heads(k * k_k)
    kk = kk / jnp.maximum(jnp.sqrt(jnp.sum(kk * kk, axis=-1, keepdims=True)), 1e-12)
    k = k * (1.0 + (a - 1.0) * k_a)
    r_h, k_h, v_h, a_h, w_h = heads(r), heads(k), heads(v), heads(a), heads(decay)

    def step(state, inp):
        r_t, w_t, k_t, v_t, aa_t, bb_t = inp
        sa = jnp.einsum('bhij,bhj->bhi', state, aa_t)
        state = (state * w_t[:, :, None, :] + sa[..., None] * bb_t[:, :, None, :]
                 + v_t[..., None] * k_t[:, :, None, :])
        y = jnp.einsum('bhij,bhj->bhi', state, r_t)
        return state, y

    xs = tuple(jnp.moveaxis(t, 1, 0) for t in (r_h, w_h, k_h, v_h, -kk, kk * a_h))
    init = jnp.zeros((b, H_B, HEAD_B, HEAD_B), jnp.float32)
    _, ys = lax.scan(step, init, xs)
    y = jnp.moveaxis(ys, 0, 1)
    mu = jnp.mean(y, axis=-1, keepdims=True)
    var = jnp.mean(jnp.square(y - mu), axis=-1, keepdims=True)
    yn = (y - mu) * lax.rsqrt(var + GN_EPS)
    gn_w = ln_x_w.reshape(H_B, HEAD_B).astype(jnp.float32)
    gn_b = ln_x_b.reshape(H_B, HEAD_B).astype(jnp.float32)
    yn = yn * gn_w + gn_b
    bonus = jnp.sum(r_h * k_h * r_k.astype(jnp.float32), axis=-1, keepdims=True) * v_h
    out = (yn + bonus) * heads(g)
    return out.reshape(b, s, W_B).astype(p.dtype)

def second_inputs(seed: int = 0) -> dict:
    key = jax.random.key(seed)
    ks = jax.random.split(key, 24)
    L = DEPTH

    def nrm(k, shape, scale):
        return jax.random.normal(k, shape, jnp.float32) * scale

    return {
        "x": nrm(ks[0], (BATCH, SEQ, D_MODEL), 1.0),
        "pre_mix_g": 1.0 + nrm(ks[1], (L, D_MODEL), 0.05),
        "w_in": nrm(ks[2], (L, D_MODEL, IN_COLS), D_MODEL ** -0.5),
        "gate_bias": nrm(ks[3], (L, GATE_COLS), 0.1),
        "rel_bias": nrm(ks[4], (L, H_A, N_REL), 0.5),
        "shift_mu": jax.random.uniform(ks[5], (L, RWKV_COLS), jnp.float32),
        "w0": jax.random.uniform(ks[6], (L, W_B), jnp.float32, -5.0, 0.5),
        "w2": nrm(ks[7], (L, DECAY_LORA, W_B), 0.1),
        "a0": nrm(ks[8], (L, W_B), 0.1),
        "a2": nrm(ks[9], (L, A_LORA, W_B), A_LORA ** -0.5),
        "g2": nrm(ks[10], (L, GATE_LORA, W_B), GATE_LORA ** -0.5),
        "k_k": 0.85 + nrm(ks[11], (L, W_B), 0.05),
        "k_a": 1.0 + nrm(ks[12], (L, W_B), 0.05),
        "r_k": nrm(ks[13], (L, H_B, HEAD_B), 0.1),
        "ln_x_w": 1.0 + nrm(ks[14], (L, W_B), 0.05),
        "ln_x_b": nrm(ks[15], (L, W_B), 0.05),
        "proj_a": nrm(ks[16], (L, W_A, D_MODEL), W_A ** -0.5),
        "proj_b": nrm(ks[17], (L, W_B, D_MODEL), W_B ** -0.5),
        "w_out": nrm(ks[18], (L, D_MODEL, D_MODEL), D_MODEL ** -0.5),
        "post_mix_g": 1.0 + nrm(ks[19], (L, D_MODEL), 0.05),
        "pre_ffn_g": 1.0 + nrm(ks[20], (L, D_MODEL), 0.05),
        "w_up": nrm(ks[21], (L, D_MODEL, D_FF), D_MODEL ** -0.5),
        "w_down": nrm(ks[22], (L, D_FF, D_MODEL), D_FF ** -0.5),
        "post_ffn_g": 1.0 + nrm(ks[23], (L, D_MODEL), 0.05),
    }

def second_block(x, pre_mix_g, w_in, gate_bias, rel_bias, shift_mu, w0, w2, a0, a2, g2,
              k_k, k_a, r_k, ln_x_w, ln_x_b, proj_a, proj_b, w_out, post_mix_g,
              pre_ffn_g, w_up, w_down, post_ffn_g):
    b, s, _ = x.shape
    for l in range(DEPTH):
        h = rms_norm(x, pre_mix_g[l])
        proj = h @ w_in[l]
        p_att = proj[..., :ATT_COLS]
        p_rwkv = proj[..., ATT_COLS:ATT_COLS + RWKV_COLS]
        p_gate = proj[..., ATT_COLS + RWKV_COLS:] + gate_bias[l]

        q, k, v = jnp.split(p_att, 3, axis=-1)
        shp = (b, s, H_A, HEAD_A)
        y_a = chunk_band_attention(q.reshape(shp), k.reshape(shp), v.reshape(shp), rel_bias[l])
        y_b = rwkv7_time_mix(p_rwkv, shift_mu[l], w0[l], w2[l], a0[l], a2[l], g2[l],
                             k_k[l], k_a[l], r_k[l], ln_x_w[l], ln_x_b[l])

        gate_a = jax.nn.sigmoid(p_gate[..., :D_MODEL])
        gate_b = jax.nn.sigmoid(p_gate[..., D_MODEL:])
        merged = gate_a * (y_a @ proj_a[l]) + gate_b * (y_b @ proj_b[l])
        x = x + rms_norm(merged @ w_out[l], post_mix_g[l])

        hf = rms_norm(x, pre_ffn_g[l])
        u = jnp.square(jax.nn.relu(hf @ w_up[l])) @ w_down[l]
        x = x + rms_norm(u, post_ffn_g[l])
    return x


def setup_inputs(seed=0):
    out = dict(first_inputs(seed))
    for name, value in second_inputs(seed + 1).items():
        if name != "x":
            out[name + "_2"] = value
    return out


def reference(
    x, norm1_w, w_in, conv_w, a_log_fwd, dt_bias_fwd, a_log_bwd, dt_bias_bwd, gdn_norm_w,
    lambda_q1, lambda_k1, lambda_q2, lambda_k2, subln_w, w_proj_attn, w_proj_gdn, w_out,
    norm2_w, w_router, w_gate, w_up, w_down, norm_f_w, pre_mix_g_2, w_in_2, gate_bias_2,
    rel_bias_2, shift_mu_2, w0_2, w2_2, a0_2, a2_2, g2_2, k_k_2, k_a_2, r_k_2, ln_x_w_2,
    ln_x_b_2, proj_a_2, proj_b_2, w_out_2, post_mix_g_2, pre_ffn_g_2, w_up_2, w_down_2,
    post_ffn_g_2,
):
    x = first_block(
        x, norm1_w, w_in, conv_w, a_log_fwd, dt_bias_fwd, a_log_bwd, dt_bias_bwd, gdn_norm_w,
        lambda_q1, lambda_k1, lambda_q2, lambda_k2, subln_w, w_proj_attn, w_proj_gdn, w_out,
        norm2_w, w_router, w_gate, w_up, w_down, norm_f_w,
    )
    return second_block(
        x, pre_mix_g_2, w_in_2, gate_bias_2, rel_bias_2, shift_mu_2, w0_2, w2_2, a0_2, a2_2,
        g2_2, k_k_2, k_a_2, r_k_2, ln_x_w_2, ln_x_b_2, proj_a_2, proj_b_2, w_out_2,
        post_mix_g_2, pre_ffn_g_2, w_up_2, w_down_2, post_ffn_g_2,
    )


_drawn_inputs = setup_inputs


def setup_inputs(seed=0):
    import zlib

    import numpy as np

    out = dict(_drawn_inputs(seed))
    spreads = {}
    factors = {'gdn_norm_w': 3.597,
     'lambda_q1': 3.628,
     'lambda_k1': 8.0,
     'subln_w': 2.994,
     'norm2_w': 2.814,
     'lambda_k2': 2.856}
    for name, (base, spread) in spreads.items():
        noise = np.random.default_rng([zlib.crc32(name.encode()), seed]).standard_normal(out[name].shape)
        drawn = base * np.exp(spread * noise) if base else spread * noise
        out[name] = __import__('jax').numpy.asarray(drawn.astype(out[name].dtype))
    for name, factor in factors.items():
        out[name] = (out[name] * factor).astype(out[name].dtype)
    return out
```

```python
import math
from contextlib import ExitStack

import numpy as np
import concourse.bass as bass
from concourse import mybir

F32 = mybir.dt.float32
F32R = mybir.dt.float32r
ALU = mybir.AluOpType
ACT = mybir.ActivationFunctionType
AX = mybir.AxisListType

P = 128
T = 512
TC = T // P
D = 1024
DC = D // P
EPS = 1e-6

AH = 8
GH = 8
HG = 4
NE = 16
FF = 2048
CAP = 2 * T // NE
LAMBDA_INIT = 0.8 - 0.6 * math.exp(-0.3 * 0)
C_Q, C_K, C_V = 0, 1024, 2048
C_G = 3072
C_Z = 6144
C_AB = 7168
C_GATE_A = 7200
C_GATE_G = 8224

WA = 512
H2 = 8
D_FF = 4096
B2_R = 3 * WA
B2_LORA = B2_R + 3 * WA
B2_GATE = B2_LORA + 256
N_REL = 320
TOE = 640
DECAY_MAX = math.exp(-0.5)
GN_EPS = 64 * 1e-5

LEVELS = 7

CONST = {}
_at = 0
for _name, _w in (("ident", P), ("ones", P), ("upto", P), ("from", P), ("rot", P), ("cos", T), ("sin", T),
                  ("lev_f", LEVELS * P), ("lev_b", LEVELS * P), ("slots", CAP), ("mask4", 4 * P),
                  ("flip", P), ("heads2", P), ("reset", T), ("pair", 2)):
    CONST[_name] = (_at, _w)
    _at += _w
CONST_W = _at


def shape_constants():
    c = np.zeros((P, CONST_W), np.float32)

    def put(name, v):
        a, w = CONST[name]
        c[:, a:a + w] = v

    i = np.arange(P)
    put("ident", np.eye(P))
    put("ones", 1.0)
    put("upto", i[:, None] <= i[None, :])
    put("from", i[:, None] >= i[None, :])
    rot = np.zeros((P, P))
    for m in range(P):
        k = m + 32 if m % 64 < 32 else m - 32
        rot[k, m] = -1.0 if m % 64 < 32 else 1.0
    put("rot", rot)
    inv = np.float32(10000.0) ** (-np.arange(0, 64, 2, dtype=np.float32) / np.float32(64))
    ang = (np.arange(T, dtype=np.float32)[:, None] * inv[None, :]).astype(np.float32)
    ang = np.concatenate([ang, ang, ang, ang], axis=1).T
    put("cos", np.cos(ang))
    put("sin", np.sin(ang))
    for lev in range(LEVELS):
        b = 2 ** lev
        odd = (i // b) % 2 == 1
        same = (i[:, None] // (2 * b)) == (i[None, :] // (2 * b))
        m = same & ~odd[:, None] & odd[None, :]
        a = CONST["lev_f"][0] + lev * P
        c[:, a:a + P] = m
        a = CONST["lev_b"][0] + lev * P
        c[:, a:a + P] = m.T
    put("slots", np.arange(CAP)[None, :])
    strict, incl = i[:, None] < i[None, :], i[:, None] <= i[None, :]
    put("mask4", np.concatenate([strict, incl, strict, incl], axis=1))
    put("flip", np.eye(P)[::-1])
    put("heads2", (i[:, None] // 64) == (i[None, :] // 64))
    put("reset", (np.arange(T) % P != 0)[None, :])
    put("pair", (i[:, None] // 64) == np.arange(2)[None, :])
    return c


VEC = {}
_at = 0
for _name, _w in (("norm1", 8), ("norm2", 8), ("subln", 1), ("gdn_norm", 1), ("conv", 24 * 5), ("pre_mix", 8),
                  ("pre_ffn", 8), ("gate_bias", 16), ("mu", 14), ("w0", 4), ("a0", 4), ("k_k", 4), ("k_a", 4),
                  ("r_k", 4)):
    VEC[_name] = (_at, _w)
    _at += _w
VEC_W = _at
ROWS = {}
_at = 0
for _name, _w in (("dt", 16), ("a_log", 16), ("lam", 256)):
    ROWS[_name] = (_at, _w)
    _at += _w
ROWS_W = _at

CHAINS = (
    "x_in 16, ln_in 16",
    "const_in 16, toe_in 16",
    "small_in 48, lora_in 32",
    "wab_in 16, g2_in 16",
    "rev_in 16, rowf_in 16",
    "ext_out 16, router_in 32",
    "w_loaded0 256, w2_loaded0 352",
    "w_loaded1 256, w2_loaded1 352",
    "w_loaded2 256, w2_loaded2 336",
    "n1_lo 8, n3_lo 8, n4_lo 8",
    "low_out 32, low2_out 32",
    "low_back 64, low2_back 32",
    "w_high 36, w2_high 37",
    "w_low 36, w2_low 37",
    "ot_out 16, x2_kept 16",
    "ot_back 16, x2_back 32",
    "x_back 16, stored 64",
    "n1_tp 8, n2_tp 8, n3_tp 8, n4_tp 8",
    "qk_proj 16, ro_logits 1, up_proj 32",
    "qk_rot 16, ro_turned 2, dn_proj 16",
    "v_proj 16, mo_gathered 16",
    "ab_proj 1, b_qk 8",
    "ab_cum 1, mo_hturned 32, b_v 8",
    "at_scores 32, mo_used 192",
    "at_turned 32, mo_turned 8",
    "at_pv 32, mo_scattered 64",
    "an_turned 8, b_scores 32",
    "gp_proj 24, b_turned 32",
    "gt_turned 24, b_pv 32",
    "gn_turned 16, b_ya_turned 4",
    "gd_gram 8, r_proj 14",
    "gd_row 16, r_low 8",
    "sc_y0 8, s_rhs 8",
    "sc_y1 8, s_sa 8",
    "sc_o0 8, s_up 6",
    "sc_su0 6, t_sum 4",
    "sc_o1 8, s_out 8",
    "sc_su1 6, t_bonus_sum 4",
    "sc_ks0 6, t_turned 12",
    "sc_ks1 6, u_scores 32",
    "z_proj 8, g_turned 4",
    "zn_sum 8, g_gate 1",
    "mg_proj 32, m2_proj 32",
    "out_proj 16, o2_proj 16",
    "n1_sq 4, n2_sq 4, n3_sq 4, n4_sq 4",
    "n1_ln 1, n2_ln 1, n3_ln 1, n4_ln 1",
    "n1_r 1, n2_r 1, n3_r 1, n4_r 1",
    "n1_ht 8, n2_ht 8, n3_ht 8, n4_ht 8",
    "qk_raw 16, ro_exp 1, m2_tanh 16",
    "v_done 16, mo_x 64, o2_copied 16",
    "lam_exp 1, b_qk_done 8, pn2_ln 1",
    "ab_exp 2, mo_he 32, b_v_done 8, pn2_r 1",
    "ab_ln 2, b_exp 32",
    "ab_decays 3, b_pt 32",
    "at_exp 64, mo_tanh 32, pn1_ln 1",
    "at_pt 32, mo_y 32, pn1_r 1",
    "an_sq 4, mo_selt 16, pn1_sq 4",
    "an_ln 1, b_yat 4",
    "an_r 1, r_copied 14",
    "an_ot 8, f1_sq 4, up_relu 32",
    "gp_copied 24, f1_ln 1, dn_copied 8",
    "gc_tanh 24, f1_r 1, pn2_sq 4",
    "gt_copied 24, r_lora 2",
    "gn_ln 2, r_gates 8",
    "gn_r 2, t_sq 4",
    "gn_back 16, t_ln 4",
    "gd_eg 16, t_rn 4",
    "gd_decay 16, t_exps 12",
    "sc_first0 4, t_tok 12",
    "sc_first1 4, t_ends_exp 3",
    "zn_sq 8, s_rhs_copied 8",
    "zn_ln 8, s_sa_copied 8",
    "zn_r 8, g_sq 1",
    "z_tanh 8, g_ln 2",
    "mg_tanh 16, g_ybt 4",
    "ext_set 3, b_masked 1",
    "eps_set 1, b_biased 32",
    "prepared 4, b_negmax 32",
    "lam_sum 1, b_rc 8",
    "n1_dg 4, n2_dg 4, n3_dg 4, n4_dg 4",
    "qk_cos 16, ro_max 1",
    "qk_sin 16, ro_shift 1",
    "qk_done 16, ro_sum 2",
    "lam_diff 2, b_o 8",
    "ab_copied 1, r_pads 1",
    "ab_t 2, r_halves 5",
    "ab_abs 1, r_diff 14",
    "ab_sp 2, r_shift 14",
    "ab_g 1, r_sig 9",
    "ab_gcc 2, t_cum 4",
    "ab_gc 1, t_kk 4",
    "ab_kd 2, t_kp 8",
    "ab_done 1, t_ends 12",
    "at_max 32, ro_aff 1",
    "at_negmax 32, ro_round 9",
    "at_rcp 32, ro_top 8",
    "at_coef 32, ro_mask 4",
    "at_pd 32, ro_slot 1",
    "at_o 8, ro_pos 2",
    "an_ss 4, t_cs 8",
    "an_scaled 4, t_bonus 4",
    "pads 1, t_max 4",
    "gc_tap 120, mo_start 4",
    "gc_silu 24, mo_pair 16",
    "gn_ss 16, mo_sel 56",
    "gn_q 2, t_norm 4",
    "gn_scaled 16, mo_s 32",
    "gd_tri 16, mo_h 32",
    "gd_diff 32, mo_acc 64",
    "gd_pt 16, x2_done 4",
    "gd_qk 16, t_ar 8",
    "sc_vn0 8, g_cent 1",
    "sc_kdv0 6, t_b 4",
    "sc_vn1 8, g_var 1",
    "sc_kdv1 6, t_hats 8",
    "sc_state0 6, u_masked 32",
    "sc_state1 6, s_state 6",
    "sc_t0 6, s_scaled 6",
    "sc_r0 6, s_y 8",
    "sc_t1 6, s_faded 4",
    "sc_r1 6, g_step 8",
    "sc_faded0 4, t_bon 1",
    "sc_faded1 4, s_grown 6",
    "sc_second0 4, g_yb 1",
    "sc_second1 4, m2_done 16",
    "zn_norm 8, m2_sum 8",
    "z_silu 8, pn1_u 4",
    "z_og 8, pn1_x 4",
    "mg_done 16, up_sq 32",
    "mg_sum 8, pn2_u 4",
    "x1_done 16, pn2_x 4",
)
CHAIN_OF = {}
for _chain in CHAINS:
    _words = _chain.replace(",", "").split()
    _sum = 0
    for _name, _total in zip(_words[0::2], _words[1::2]):
        CHAIN_OF[_name] = (_words[0], _sum)
        _sum += int(_total)

M_CONST = 0
M_VEC = CONST_W
M_ROWS = M_VEC + VEC_W
M_SMALL = M_ROWS + ROWS_W
M_X = (M_SMALL + 1830) // 8 * 8
M_HT = M_X + TC * D
M_RING = M_HT + DC * T
SLOT = DC * 256
SLOTS = 3
M_HI = M_RING + 2 * SLOT
M_DYN = M_HI + 2 * SLOT
M_END = M_DYN + 29696


def build_program(nc, a):
    ctx = ExitStack()
    with ctx:
        sbuf_at = (nc.sbuf_base + 127) // 128 * 128
        S = nc.alloc_sbuf_tensor_at("S", [P, M_END], F32, offset=sbuf_at)
        PS = ctx.enter_context(nc.psum_tensor("PS", [P, 8, 512], F32))
        sems = {}

        def sem(name):
            first = CHAIN_OF.get(name, (name, 0))[0]
            if first not in sems:
                sems[first] = ctx.enter_context(nc.semaphore(first))
            return sems[first]

        def count(name, value):
            return sem(name), value + CHAIN_OF.get(name, (name, 0))[1]

        def at(off, *shape):
            n = 1
            for s in shape:
                n *= s
            v = S[:, off:off + n]
            if len(shape) == 2:
                v = v.rearrange("p (a b) -> p a b", a=shape[0])
            elif len(shape) == 3:
                v = v.rearrange("p (a b c) -> p a b c", a=shape[0], b=shape[1])
            return v

        def const(name):
            o, w = CONST[name]
            return S[:, M_CONST + o:M_CONST + o + w]

        def vec(name, j=0, n=1):
            o = M_VEC + VEC[name][0] + j
            return S[:, o:o + n]

        def row(name):
            o, w = ROWS[name]
            return S[:, M_ROWS + o:M_ROWS + o + w]

        small_at = [M_SMALL]

        def small(*shape):
            n = 1
            for s in shape:
                n *= s
            o = small_at[0]
            small_at[0] += n
            assert small_at[0] <= M_X
            return at(o, *shape)

        def spread(col, n):
            return col.unsqueeze(2).to_broadcast([P, col.shape[1], n])

        def every(m, k):
            return m.unsqueeze(1).to_broadcast([P, k, m.shape[1]])

        def grid(v, k):
            return v.rearrange("p (a b) -> p a b", a=k)

        ident, ones = const("ident"), const("ones")
        X = at(M_X, TC, D)
        HT = at(M_HT, DC, T)
        WH = [at(M_HI + s * SLOT, DC, 256) for s in range(2)]

        eps = small(1)
        ss = small(TC)
        lnv = small(TC)
        rs = small(TC)
        diag = small(TC, P)
        nlam = small(1)
        lam_e = small(2)
        scratch_at = small_at[0]
        lam_p = small(2, 64)
        half_conv = small(24 * 5)
        sub_scaled = small(1)
        gdn_half = small(1)
        wab = small(DC, 32)
        ab = small(TC, 32)
        Gd = small(TC, 16)
        tmp16 = small(TC, 16)
        tmp16b = small(TC, 16)
        nexp_a = small(16)
        BETA = small(TC, 16)
        GC = small(2, TC, 8)
        GLAST = small(TC, 16)
        NEG_EG = small(2, TC, 8)
        KD = small(2, TC, 8)
        GL = small(TC, 16)
        rnorm = small(8, TC)
        rnorm_l = small(8, TC)

        ot_dram = nc.dram_tensor("attention_out", (P, 8 * T), F32, kind="Internal").ap()

        def cols(w, c):
            return w[0, :, c:c + 256].rearrange("(dc p) n -> p dc n", p=P)

        loads = []
        where = {}
        HTL = at(M_DYN + 16384, DC, T)
        htl_dram = nc.dram_tensor("low_parts", (P, DC * T), F32, kind="Internal").ap()

        def load(name, src, done, value):
            where[name] = len(loads)
            loads.append((src, done, value))

        for j in range(8):
            load(("qk", j), cols(a["w_in"], C_Q + 256 * j), "qk_proj", 2 * (j + 1))
        for j in range(4):
            load(("v", j), cols(a["w_in"], C_V + 256 * j), "v_proj", 4 * (j + 1))
        for gr in range(2):
            for j in range(6):
                c = C_G + 1024 * (j // 2) + gr * 512 + 256 * (j % 2)
                load(("g", gr, j), cols(a["w_in"], c), "gp_proj", 12 * gr + 2 * (j + 1))
        for j in range(4):
            load(("z", j), cols(a["w_in"], C_Z + 256 * j), "z_proj", 2 * (j + 1))
        for k in range(4):
            for m, (w, c) in enumerate(((a["w_proj_attn"], 0), (a["w_proj_gdn"], 0),
                                        (a["w_in"], C_GATE_A), (a["w_in"], C_GATE_G))):
                load(("m", k, m), cols(w, c + 256 * k), "mg_proj", 8 * k + 2 * (m + 1))
        for j in range(4):
            load(("o", j), cols(a["w_out"], 256 * j), "out_proj", 4 * (j + 1))

        def slot_of(name):
            n = where[name]
            third = M_DYN + (12288 if n < where[("m", 0, 0)] else 26624)
            return at(third if n % SLOTS == 2 else M_RING + (n % SLOTS) * SLOT, DC, 256)

        def await_slot(eng, name):
            n = where[name]
            eng.wait_ge(*count(f"w_loaded{n % SLOTS}", 16 * (n // SLOTS + 1)))

        splits = [n for n in where if n[0] in ("qk", "v", "g", "z") or (n[0] == "m" and n[2] >= 2)]
        turn_of = {n: k for k, n in enumerate(splits)}

        r_blocks = {}

        def r32(v):
            g, o = divmod(v.offset - M_HT, SLOT)
            if g not in r_blocks:
                r_blocks[g] = nc.alloc_sbuf_tensor_at(f"r_block{g}", [P, SLOT], F32R, offset=sbuf_at + 4 * (M_HT + g * SLOT))
            return bass.AP(r_blocks[g][:, 0:1].tensor, o, [[SLOT, P]] + [list(d) for d in v.ap[1:]])

        def rounded(v):
            return r32(v).bitcast(F32)

        def after(name):
            k = turn_of[name] + 1
            if k < len(splits) and splits[k][0] == name[0] and (name[0] != "g" or splits[k][1] == name[1]):
                return splits[k]
            return None

        def half_at(o, s):
            return at(o + s * SLOT, SLOT)

        def split_act(act, name):
            if name is None:
                return
            k = turn_of[name]
            await_slot(act, name)
            if k >= 2:
                _, done, value = loads[where[splits[k - 2]]]
                act.wait_ge(*count(done, value))
            act.activation(r32(WH[k % 2]), slot_of(name), ACT.Copy).then_inc(sem("w_high"), 1)

        def split_pool(pool, name):
            if name is None:
                return
            k = turn_of[name]
            pool.wait_ge(*count("w_high", k + 1))
            w = slot_of(name)
            pool.tensor_tensor(r32(w), w, rounded(WH[k % 2]), ALU.subtract).then_inc(sem("w_low"), 1)

        def await_split(pe, name):
            pe.wait_ge(*count("w_low", turn_of[name] + 1))

        def parts_of(name):
            return WH[turn_of[name] % 2], slot_of(name)

        def norm_act(act, tag, ready, weight):
            for tc in range(TC):
                for s, v in ready:
                    if tag in ("n3", "n4"):
                        act.wait_ge(*count(s, v - TC + tc + 1))
                    elif tc == 0:
                        act.wait_ge(*count(s, v))
                act.activation(HT[:, 2 * tc:2 * tc + 2, :], grid(X[:, tc, :], 2), ACT.Square,
                               accum_out=ss[:, tc:tc + 1]).then_inc(sem(tag + "_sq"), 1)
            act.wait_ge(*count(tag + "_sq", TC))
            act.activation(lnv, ss, ACT.Ln, bias=eps, scale=1.0 / D).then_inc(sem(tag + "_ln"), 1)
            act.wait_ge(*count(tag + "_ln", 1))
            act.activation(rs, lnv, ACT.Exp, scale=-0.5).then_inc(sem(tag + "_r"), 1)
            for dc in range(DC):
                act.wait_ge(*count(tag + "_tp", dc + 1))
                out = HT[:, dc, :] if tag == "n2" else r32(HT[:, dc, :])
                act.activation(out, PS[:, dc % 2, :], ACT.Copy, scale=vec(weight, dc)).then_inc(sem(tag + "_ht"), 1)

        def norm_dve(dve, tag):
            dve.wait_ge(*count(tag + "_r", 1))
            for tc in range(TC):
                dve.tensor_scalar(diag[:, tc, :], ident, rs[:, tc:tc + 1], None, ALU.mult)\
                    .then_inc(sem(tag + "_dg"), 1)

        def norm_low_dve(dve, tag, low, weight):
            for dc in range(DC):
                dve.wait_ge(*count(tag + "_ht", dc + 1))
                dve.scalar_tensor_tensor(r32(low[:, dc, :]), PS[:, dc % 2, :], vec(weight, dc), rounded(HT[:, dc, :]),
                                         ALU.mult, ALU.subtract).then_inc(sem(tag + "_lo"), 1)

        def norm_pe(pe, tag):
            pe.wait_ge(*count(tag + "_dg", TC))
            for dc in range(DC):
                if dc >= 2:
                    pe.wait_ge(*count(tag + ("_ht" if tag == "n2" else "_lo"), dc - 1))
                for tc in range(TC):
                    mm = pe.matmul(PS[:, dc % 2, tc * P:(tc + 1) * P], X[:, tc, dc * P:(dc + 1) * P],
                                   diag[:, tc, :], start=True, stop=True)
                mm.then_inc(sem(tag + "_tp"), 1)

        def feature_tile(pe, out, w, off, src):
            for dc in range(DC):
                mm = pe.matmul(out, w[:, dc, off:off + P], src[:, dc, :], start=(dc == 0), stop=(dc == DC - 1))
            return mm

        def split_tile(pe, out, w, off, low):
            high_w, low_w = w
            for dc in range(DC):
                wh, wl = (r32(v[:, dc, off:off + P]) for v in (high_w, low_w))
                pe.matmul(out, wh, r32(HT[:, dc, :]), start=(dc == 0), stop=False)
                pe.matmul(out, wh, r32(low[:, dc, :]), start=False, stop=False)
                mm = pe.matmul(out, wl, r32(HT[:, dc, :]), start=False, stop=(dc == DC - 1))
            return mm

        def split_token_tile(pe, out, w, low, tc):
            high_w, low_w = w
            s = slice(tc * P, (tc + 1) * P)
            for dc in range(DC):
                hi = r32(HT[:, dc, s])
                pe.matmul(out, hi, r32(high_w[:, dc, :]), start=(dc == 0), stop=False)
                pe.matmul(out, hi, r32(low_w[:, dc, :]), start=False, stop=False)
                mm = pe.matmul(out, r32(low[:, dc, s]), r32(high_w[:, dc, :]), start=False, stop=(dc == DC - 1))
            return mm

        def token_tile(pe, out, w, src, tc):
            for dc in range(DC):
                mm = pe.matmul(out, src[:, dc, tc * P:(tc + 1) * P], w[:, dc, :],
                               start=(dc == 0), stop=(dc == DC - 1))
            return mm

        QT = at(M_DYN, 8, T)
        KT = at(M_DYN + 4096, 8, T)
        V = at(M_DYN + 8192, TC, D)
        OA = at(M_DYN + 12288, TC, D)
        A0 = M_DYN + 20480
        qk_raw = at(A0, 2, T)
        qk_tmp = at(A0 + 1024, 2, T)
        pr = at(A0 + 2048, 2, 2, T)
        pd = at(A0 + 4096, 2, T)
        pT = at(A0 + 5120, 2, T)
        mx = at(A0 + 6144, 4, 2)
        nmx = at(A0 + 6152, 4, 2)
        sums = at(A0 + 6160, 32, 2)
        rcp = at(A0 + 6224, 32, 2)
        coef = at(A0 + 6288, 32)
        oss = at(A0 + 6320, TC, 8)
        oln = at(A0 + 6352, TC, 8)
        ors = at(A0 + 6384, TC, 8)
        OT = QT
        QK = [QT[:, h, :] for h in range(8)] + [KT[:, h, :] for h in range(8)]
        A_STEPS = AH * TC
        A_SCALE = 64 ** -0.5

        def attention_pe(pe):
            pe.wait_ge(*count("n1_lo", DC))

            def rotate(p):
                pe.wait_ge(*count("qk_raw", p + 1))
                if p >= 2:
                    pe.wait_ge(*count("qk_sin", p - 1))
                pe.matmul(PS[:, 2 + p % 2, :], const("rot"), qk_raw[:, p % 2, :], start=True, stop=True)\
                    .then_inc(sem("qk_rot"), 1)

            for p in range(16):
                if p % 2 == 0:
                    await_split(pe, ("qk", p // 2))
                if p >= 2:
                    pe.wait_ge(*count("qk_raw", p - 1))
                split_tile(pe, PS[:, p % 2, :], parts_of(("qk", p // 2)), P * (p % 2), HTL)\
                    .then_inc(sem("qk_proj"), 1)
                if p:
                    rotate(p - 1)
            rotate(15)
            for p in range(16):
                j, tc = p // 4, p % 4
                if tc == 0:
                    await_split(pe, ("v", j))
                if p < 2:
                    pe.wait_ge(*count("qk_raw", 16))
                else:
                    pe.wait_ge(*count("v_done", p - 1))
                split_token_tile(pe, PS[:, p % 2, 0:256], parts_of(("v", j)), HTL, tc).then_inc(sem("v_proj"), 1)
            pe.wait_ge(*count("v_done", 16))
            pe.wait_ge(*count("wab_in", 16))
            for tc in range(TC):
                for n, src in enumerate((HT, HTL)):
                    for dc in range(DC):
                        mm = pe.matmul(PS[:, 4, tc * 32:(tc + 1) * 32], rounded(src[:, dc, tc * P:(tc + 1) * P]), wab[:, dc, :],
                                       start=(n == 0 and dc == 0), stop=(n == 1 and dc == DC - 1))
            mm.then_inc(sem("ab_proj"), 1)
            pe.wait_ge(*count("ab_g", 1))
            pe.wait_ge(*count("ab_copied", 1))
            pe.matmul(PS[:, 4, 0:64], const("upto"), Gd.rearrange("p a b -> p (a b)"), start=True, stop=True)
            pe.matmul(PS[:, 4, 64:128], const("from"), Gd.rearrange("p a b -> p (a b)"), start=True, stop=True)
            pe.matmul(PS[:, 4, 128:192], ones, Gd.rearrange("p a b -> p (a b)"), start=True, stop=True)\
                .then_inc(sem("ab_cum"), 1)

            def scores(i):
                h, qc, b = i // TC, i % TC, 2 * (i % 2)
                if i == 0:
                    pe.wait_ge(*count("qk_done", 16))
                    pe.wait_ge(*count("qk_sin", 16))
                if i >= 2:
                    pe.wait_ge(*count("at_exp", 2 * (i - 1)))
                for t in range(2):
                    s = slice(64 * t, 64 * t + 64)
                    mm = pe.matmul(PS[:, b + t, :], QT[s, h, qc * P:(qc + 1) * P], KT[s, h, :],
                                   start=True, stop=True)
                mm.then_inc(sem("at_scores"), 1)

            def turn(i):
                pe.wait_ge(*count("at_pd", i + 1))
                if i < 2:
                    pe.wait_ge(*count("ab_done", 1))
                else:
                    pe.wait_ge(*count("at_pt", i - 1))
                for kc in range(TC):
                    mm = pe.transpose(PS[:, 4 + i % 2, kc * P:(kc + 1) * P], pd[:, i % 2, kc * P:(kc + 1) * P], ident)
                mm.then_inc(sem("at_turned"), 1)

            def values(i):
                h, qc = i // TC, i % TC
                pe.wait_ge(*count("at_pt", i + 1))
                if qc == 0 and h >= 2:
                    pe.wait_ge(*count("at_o", h - 1))
                for kc in range(TC):
                    mm = pe.matmul(PS[:, 6 + h % 2, qc * P:(qc + 1) * P], pT[:, i % 2, kc * P:(kc + 1) * P],
                                   V[:, kc, h * P:(h + 1) * P], start=(kc == 0), stop=(kc == TC - 1))
                mm.then_inc(sem("at_pv"), 1)

            for s in range(A_STEPS + 3):
                if s < A_STEPS:
                    scores(s)
                if 2 <= s <= A_STEPS + 1:
                    turn(s - 2)
                if s >= 3:
                    values(s - 3)
            pe.wait_ge(*count("at_exp", 2 * A_STEPS))
            for h in range(AH):
                if h == 0:
                    pe.wait_ge(*count("an_scaled", TC))
                if h >= 2:
                    pe.wait_ge(*count("an_ot", h - 1))
                for tc in range(TC):
                    mm = pe.transpose(PS[:, h % 2, tc * P:(tc + 1) * P], OA[:, tc, h * P:(h + 1) * P], ident)
                mm.then_inc(sem("an_turned"), 1)

        def attention_pool(pool):
            for kind, n in (("qk", 8), ("v", 4)):
                for j in range(n):
                    split_pool(pool, (kind, j))

        def attention_act(act):
            for p in range(16):
                if p % 2 == 0:
                    split_act(act, after(("qk", p // 2)) or ("v", 0))
                act.wait_ge(*count("qk_proj", p + 1))
                if p >= 2:
                    act.wait_ge(*count("qk_rot", p - 1))
                    act.wait_ge(*count("qk_cos", p - 1))
                act.activation(qk_raw[:, p % 2, :], PS[:, p % 2, :], ACT.Copy).then_inc(sem("qk_raw"), 1)
            for p in range(16):
                j, tc = p // 4, p % 4
                if tc == 0:
                    split_act(act, after(("v", j)))
                act.wait_ge(*count("v_proj", p + 1))
                act.activation(V[:, tc, 256 * j:256 * (j + 1)], PS[:, p % 2, 0:256], ACT.Copy)\
                    .then_inc(sem("v_done"), 1)
            act.wait_ge(*count("lam_sum", 1))
            act.activation(lam_e, lam_e, ACT.Exp).then_inc(sem("lam_exp"), 1)
            act.wait_ge(*count("ab_abs", 1))
            act.activation(nexp_a, row("a_log"), ACT.Exp).then_inc(sem("ab_exp"), 1)
            act.activation(tmp16b, tmp16, ACT.Exp, scale=-1.0).then_inc(sem("ab_exp"), 1)
            act.wait_ge(*count("ab_exp", 2))
            act.activation(tmp16b, tmp16b, ACT.Ln, bias=1.0).then_inc(sem("ab_ln"), 1)
            act.activation(BETA, ab[:, :, 16:32], ACT.Tanh, scale=0.5).then_inc(sem("ab_ln"), 1)
            act.wait_ge(*count("ab_gc", 1))
            act.activation(NEG_EG, GC, ACT.Exp).then_inc(sem("ab_decays"), 1)
            act.activation(GL, GLAST, ACT.Exp).then_inc(sem("ab_decays"), 1)
            act.wait_ge(*count("ab_kd", 2))
            act.activation(KD, KD, ACT.Exp).then_inc(sem("ab_decays"), 1)

            def exps(i):
                act.wait_ge(*count("at_negmax", i + 1))
                if i >= 2:
                    act.wait_ge(*count("at_pd", i - 1))
                for t in range(2):
                    act.activation(pr[:, i % 2, t, :], PS[:, 2 * (i % 2) + t, :], ACT.Exp,
                                   bias=nmx[:, i % 4, t:t + 1], scale=A_SCALE,
                                   accum_out=sums[:, i, t:t + 1]).then_inc(sem("at_exp"), 1)

            def copy_turned(i):
                act.wait_ge(*count("at_turned", i + 1))
                if i >= 2:
                    act.wait_ge(*count("at_pv", i - 1))
                act.activation(pT[:, i % 2, :], PS[:, 4 + i % 2, :], ACT.Copy).then_inc(sem("at_pt"), 1)

            for s in range(A_STEPS + 2):
                if s < A_STEPS:
                    exps(s)
                if s >= 2:
                    copy_turned(s - 2)
            act.wait_ge(*count("at_o", AH))
            for tc in range(TC):
                act.activation(at(M_DYN + 4096 + 1024 * tc, D), OA[:, tc, :], ACT.Square).then_inc(sem("an_sq"), 1)
            act.wait_ge(*count("an_ss", TC))
            act.activation(oln, oss, ACT.Ln, bias=eps, scale=1.0 / P).then_inc(sem("an_ln"), 1)
            act.wait_ge(*count("an_ln", 1))
            act.activation(ors, oln, ACT.Exp, scale=-0.5).then_inc(sem("an_r"), 1)
            act.wait_ge(*count("prepared", 4))
            for h in range(AH):
                act.wait_ge(*count("an_turned", h + 1))
                act.activation(OT[:, h, :], PS[:, h % 2, :], ACT.Copy, scale=sub_scaled).then_inc(sem("an_ot"), 1)

        def prepare_dve(dve):
            dve.memset(eps, EPS).then_inc(sem("eps_set"), 1)
            dve.wait_ge(*count("small_in", 48))
            dve.tensor_scalar(half_conv, vec("conv", 0, 120), 0.5, None, ALU.mult).then_inc(sem("prepared"), 1)
            dve.tensor_scalar(sub_scaled, vec("subln"), 1.0 - LAMBDA_INIT, None, ALU.mult).then_inc(sem("prepared"), 1)
            dve.tensor_scalar(gdn_half, vec("gdn_norm"), 0.5, None, ALU.mult).then_inc(sem("prepared"), 1)
            lv = grid(row("lam"), 4)
            dve.tensor_tensor(lam_p, lv[:, 0:4:2, :], lv[:, 1:4:2, :], ALU.mult).then_inc(sem("prepared"), 1)
            dve.wait_ge(*count("prepared", 4))
            dve.tensor_reduce(lam_e, lam_p, AX.X, ALU.add).then_inc(sem("lam_sum"), 1)

        def attention_dve(dve):
            def sine(p):
                dve.wait_ge(*count("qk_rot", p + 1))
                dve.tensor_tensor(qk_tmp[:, p % 2, :], PS[:, 2 + p % 2, :], const("sin"), ALU.mult)\
                    .then_inc(sem("qk_sin"), 1)
                dve.wait_ge(*count("qk_sin", p + 1))
                dve.tensor_tensor(QK[p], QK[p], qk_tmp[:, p % 2, :], ALU.add).then_inc(sem("qk_done"), 1)

            for p in range(16):
                dve.wait_ge(*count("qk_raw", p + 1))
                dve.tensor_tensor(QK[p], qk_raw[:, p % 2, :], const("cos"), ALU.mult).then_inc(sem("qk_cos"), 1)
                if p == 0:
                    continue
                dve.wait_ge(*count("qk_cos", p))
                sine(p - 1)
            dve.wait_ge(*count("qk_cos", 16))
            sine(15)
            dve.wait_ge(*count("lam_exp", 1))
            dve.tensor_tensor(nlam, lam_e[:, 1:2], lam_e[:, 0:1], ALU.subtract).then_inc(sem("lam_diff"), 1)
            dve.wait_ge(*count("lam_diff", 1))
            dve.tensor_scalar(nlam, nlam, -LAMBDA_INIT, None, ALU.add).then_inc(sem("lam_diff"), 1)
            dve.wait_ge(*count("ab_proj", 1))
            dve.tensor_copy(ab, grid(PS[:, 4, 0:128], TC)).then_inc(sem("ab_copied"), 1)
            dve.wait_ge(*count("ab_copied", 1))
            dve.tensor_tensor(ab[:, :, 0:16], ab[:, :, 0:16], every(row("dt"), TC), ALU.add).then_inc(sem("ab_t"), 1)
            dve.wait_ge(*count("ab_t", 1))
            dve.tensor_scalar(tmp16, ab[:, :, 0:16], -1.0, None, ALU.mult).then_inc(sem("ab_t"), 1)
            dve.wait_ge(*count("ab_t", 2))
            dve.tensor_tensor(tmp16, tmp16, ab[:, :, 0:16], ALU.max).then_inc(sem("ab_abs"), 1)
            dve.wait_ge(*count("ab_ln", 2))
            dve.scalar_tensor_tensor(tmp16, ab[:, :, 0:16], 0.0, tmp16b, ALU.max, ALU.add).then_inc(sem("ab_sp"), 1)
            dve.tensor_scalar(BETA, BETA, 0.5, 0.5, ALU.mult, ALU.add).then_inc(sem("ab_sp"), 1)
            dve.wait_ge(*count("ab_sp", 2))
            dve.scalar_tensor_tensor(Gd, tmp16, -1.0, every(nexp_a, TC), ALU.mult, ALU.mult).then_inc(sem("ab_g"), 1)
            dve.wait_ge(*count("ab_cum", 1))
            cum = PS[:, 4, 0:192].rearrange("p (k c h) -> p k c h", k=3, c=TC)
            dve.tensor_copy(GC[:, 0, :, :], cum[:, 0, :, 0:8]).then_inc(sem("ab_gcc"), 1)
            dve.tensor_copy(GC[:, 1, :, :], cum[:, 1, :, 8:16]).then_inc(sem("ab_gcc"), 1)
            dve.wait_ge(*count("ab_gcc", 2))
            dve.tensor_copy(GLAST, cum[:, 2, :, :]).then_inc(sem("ab_gc"), 1)
            dve.wait_ge(*count("ab_gc", 1))
            for d in range(2):
                dve.tensor_tensor(KD[:, d, :, :], GLAST[:, :, 8 * d:8 * d + 8], GC[:, d, :, :], ALU.subtract)\
                    .then_inc(sem("ab_kd"), 1)
            dve.wait_ge(*count("ab_decays", 1))
            dve.tensor_scalar(NEG_EG, NEG_EG, -1.0, None, ALU.mult).then_inc(sem("ab_done"), 1)
            dve.wait_ge(*count("lam_diff", 2))

            def maxima(i):
                b = 2 * (i % 2)
                dve.wait_ge(*count("at_scores", i + 1))
                dve.tensor_reduce(mx[:, i % 4, :], PS[:, b:b + 2, :], AX.X, ALU.max).then_inc(sem("at_max"), 1)
                dve.wait_ge(*count("at_max", i + 1))
                dve.tensor_scalar(nmx[:, i % 4, :], mx[:, i % 4, :], -A_SCALE, None, ALU.mult)\
                    .then_inc(sem("at_negmax"), 1)

            def mix(i):
                dve.wait_ge(*count("at_exp", 2 * (i + 1)))
                dve.reciprocal(rcp[:, i, :], sums[:, i, :]).then_inc(sem("at_rcp"), 1)
                dve.wait_ge(*count("at_rcp", i + 1))
                dve.scalar_tensor_tensor(coef[:, i:i + 1], sums[:, i, 0:1], nlam, rcp[:, i, 1:2],
                                         ALU.mult, ALU.mult).then_inc(sem("at_coef"), 1)
                dve.wait_ge(*count("at_coef", i + 1))
                if i >= 2:
                    dve.wait_ge(*count("at_turned", i - 1))
                dve.scalar_tensor_tensor(pd[:, i % 2, :], pr[:, i % 2, 1, :], coef[:, i:i + 1], pr[:, i % 2, 0, :],
                                         ALU.mult, ALU.add).then_inc(sem("at_pd"), 1)

            def output(h):
                dve.wait_ge(*count("at_pv", TC * (h + 1)))
                dve.tensor_tensor(OA[:, :, h * P:(h + 1) * P], grid(PS[:, 6 + h % 2, :], TC),
                                  rcp[:, TC * h:TC * h + TC, 0:1].to_broadcast([P, TC, P]), ALU.mult)\
                    .then_inc(sem("at_o"), 1)

            for s in range(A_STEPS + 2):
                if s >= 2:
                    mix(s - 2)
                if s < A_STEPS:
                    maxima(s)
                if s >= 8 and (s - 8) % TC == 0:
                    output((s - 8) // TC)
            output(AH - 1)
            for tc in range(TC):
                dve.wait_ge(*count("an_sq", tc + 1))
                dve.tensor_reduce(oss[:, tc, :], at(M_DYN + 4096 + 1024 * tc, AH, P), AX.X, ALU.add)\
                    .then_inc(sem("an_ss"), 1)
            dve.wait_ge(*count("an_r", 1))
            for tc in range(TC):
                o = grid(OA[:, tc, :], AH)
                dve.tensor_tensor(o, o, spread(ors[:, tc, :], P), ALU.mult).then_inc(sem("an_scaled"), 1)

        RAW = at(M_DYN, 12, T)
        TOK = at(M_DYN + 6144, 12, T)
        XTD = [at(M_DYN + 12288 + 2048 * d, HG, T) for d in range(2)]
        QKD = [at(M_DYN + 16384 + 2048 * d, HG, T) for d in range(2)]
        G0 = M_DYN + 20480
        OG = at(M_X, GH, T)

        def inverse_buffers(base):
            return [dict(X=at(base + 2048 * d, T), U=at(base + 2048 * d + 512, T), PT=at(base + 2048 * d + 1024, T),
                         LT=at(base + 2048 * d + 1536, T)) for d in range(2)]

        INV = inverse_buffers(G0)
        SC = [dict(S=at(G0 + 2048 * d, T), R=at(G0 + 2048 * d + 512, T), VN=at(G0 + 2048 * d + 1024, T),
                   KDV=at(G0 + 2048 * d + 1536, T)) for d in range(2)]
        GT = at(G0 + 4096, 2, T)
        DE = at(G0 + 5120, 2, T)
        EGR = at(G0 + 6144, 2, T)
        PB = at(G0 + 7168, 2, T + 4)
        ACC = at(G0, 2, T)
        TH = at(G0 + 1024, 2, T)
        SQ = at(G0 + 2048, 2, T)
        upto = {0: const("upto"), 1: const("from")}
        lev_f, lev_b = grid(const("lev_f"), LEVELS), grid(const("lev_b"), LEVELS)

        def block_of(c):
            return slice(c * P, (c + 1) * P)

        def inverse_pool(pool, q, lanes, masks):
            for lev in range(LEVELS):
                for d in range(2):
                    if q < GH:
                        pool.wait_ge(*count(f"inv_pt{d}", q + 1))
                    if lev >= 1:
                        pool.wait_ge(*count(f"inv_u{d}", 7 * q + lev))
                        pool.wait_ge(*count(f"inv_x{d}", 13 * q + 2))
                    elif q:
                        pool.wait_ge(*count(f"inv_u{d}", 7 * q))
                    pool.tensor_tensor(grid(lanes[d]["LT"], TC), grid(lanes[d]["PT"], TC),
                                       every(masks[d][:, lev, :], TC), ALU.mult).then_inc(sem(f"inv_lt{d}"), 1)

        def inverse_pe(pe, q, lanes, XT):
            for lev in range(LEVELS):
                for d in range(2):
                    b, w = 2 + 3 * d, lanes[d]
                    pe.wait_ge(*count(f"inv_lt{d}", 7 * q + lev + 1))
                    if lev:
                        pe.wait_ge(*count(f"inv_x{d}", 13 * q + 2 * lev - 1))
                    for c in range(TC):
                        s = block_of(c)
                        if lev == 0:
                            mm = pe.transpose(PS[:, b, s], w["LT"][:, s], ident)
                        else:
                            mm = pe.matmul(PS[:, b, s], w["LT"][:, s], w["X"][:, s], start=True, stop=True)
                    mm.then_inc(sem(f"inv_u{d}"), 1)
                for d in range(2):
                    b, w = 2 + 3 * d, lanes[d]
                    if lev == 0:
                        continue
                    pe.wait_ge(*count(f"inv_x{d}", 13 * q + 2 * lev))
                    pe.wait_ge(*count(f"inv_usb{d}", 6 * q + lev))
                    for c in range(TC):
                        s = block_of(c)
                        if lev < LEVELS - 1:
                            pe.matmul(PS[:, b + 1, s], XT[d][:, s], w["U"][:, s], start=True, stop=True)
                        mm = pe.matmul(PS[:, b + 2, s], w["U"][:, s], XT[d][:, s], start=True, stop=True)
                    mm.then_inc(sem(f"inv_a{d}"), 1)

        def inverse_act(act, q, lanes):
            for lev in range(1, LEVELS):
                for d in range(2):
                    act.wait_ge(*count(f"inv_u{d}", 7 * q + lev + 1))
                    act.activation(lanes[d]["U"], PS[:, 2 + 3 * d, :], ACT.Copy).then_inc(sem(f"inv_usb{d}"), 1)

        def inverse_dve(dve, q, lanes, XT):
            for lev in range(LEVELS):
                for d in range(2):
                    b, w = 2 + 3 * d, lanes[d]
                    if lev == 0:
                        dve.wait_ge(*count(f"inv_u{d}", 7 * q + 1))
                        dve.tensor_tensor(grid(w["X"], TC), every(ident, TC), grid(PS[:, b, :], TC), ALU.subtract)\
                            .then_inc(sem(f"inv_x{d}"), 1)
                        dve.tensor_tensor(grid(XT[d], TC), every(ident, TC), grid(w["LT"], TC), ALU.subtract)\
                            .then_inc(sem(f"inv_x{d}"), 1)
                        continue
                    dve.wait_ge(*count(f"inv_a{d}", 6 * q + lev))
                    if lev < LEVELS - 1:
                        dve.tensor_tensor(w["X"], w["X"], PS[:, b + 1, :], ALU.subtract).then_inc(sem(f"inv_x{d}"), 1)
                    dve.tensor_tensor(XT[d], XT[d], PS[:, b + 2, :], ALU.subtract).then_inc(sem(f"inv_x{d}"), 1)

        def group_pe(pe, gr):
            def to_tokens(gi):
                pe.wait_ge(*count("gc_silu", gi + 1))
                if gi >= 2:
                    pe.wait_ge(*count("gt_copied", gi - 1))
                for c in range(TC):
                    mm = pe.transpose(PS[:, 2 + gi % 2, block_of(c)], RAW[:, gi % 12, block_of(c)], ident)
                mm.then_inc(sem("gt_turned"), 1)

            for j in range(12):
                gi = 12 * gr + j
                if j % 2 == 0:
                    if gr and j == 0:
                        pe.wait_ge(*count("low_back", 32))
                    await_split(pe, ("g", gr, j // 2))
                if gi >= 2:
                    pe.wait_ge(*count("gp_copied", gi - 1))
                split_tile(pe, PS[:, gi % 2, :], parts_of(("g", gr, j // 2)), P * (j % 2), HTL)\
                    .then_inc(sem("gp_proj"), 1)
                if j >= 2:
                    to_tokens(gi - 2)
            to_tokens(12 * gr + 10)
            to_tokens(12 * gr + 11)
            for j in range(8):
                pe.wait_ge(*count("gn_scaled", 8 * gr + j + 1))
                if j >= 2:
                    pe.wait_ge(*count("gn_back", 8 * gr + j - 1))
                for c in range(TC):
                    mm = pe.transpose(PS[:, 4 + j % 2, block_of(c)], TOK[:, j, block_of(c)], ident)
                mm.then_inc(sem("gn_turned"), 1)

        def group_act(act, gr):
            if gr == 0:
                split_act(act, ("g", 0, 0))
            for j in range(12 + 2):
                gi = 12 * gr + j
                if j < 12:
                    if j % 2 == 0:
                        split_act(act, after(("g", gr, j // 2)))
                    act.wait_ge(*count("gp_proj", gi + 1))
                    act.wait_ge(*count("pads", 1))
                    if gi >= 2:
                        act.wait_ge(*count("gc_tap", 5 * (gi - 1)))
                    act.activation(PB[:, gi % 2, 2:2 + T], PS[:, gi % 2, :], ACT.Copy).then_inc(sem("gp_copied"), 1)
                if 1 <= j <= 12:
                    act.wait_ge(*count("gc_tap", 5 * gi))
                    if gi >= 3:
                        act.wait_ge(*count("gc_silu", gi - 2))
                    act.activation(TH[:, (gi - 1) % 2, :], ACC[:, (gi - 1) % 2, :], ACT.Tanh).then_inc(sem("gc_tanh"), 1)
                if j >= 2:
                    act.wait_ge(*count("gt_turned", gi - 1))
                    act.activation(TOK[:, j - 2, :], PS[:, 2 + (gi - 2) % 2, :], ACT.Copy).then_inc(sem("gt_copied"), 1)
            act.wait_ge(*count("gn_ss", 8 * (gr + 1)))
            act.activation(rnorm_l, rnorm, ACT.Ln, bias=eps).then_inc(sem("gn_ln"), 1)
            act.wait_ge(*count("gn_ln", gr + 1))
            act.activation(rnorm, rnorm_l, ACT.Exp, scale=-0.5).then_inc(sem("gn_r"), 1)
            for j in range(8):
                act.wait_ge(*count("gn_turned", 8 * gr + j + 1))
                act.activation(RAW[:, j, :], PS[:, 4 + j % 2, :], ACT.Copy).then_inc(sem("gn_back"), 1)

        def group_dve(dve, gr):
            def sum_squares(j):
                n = 8 * gr + j
                dve.wait_ge(*count("gn_sq", n + 1))
                dve.tensor_reduce(rnorm[:, j, :], grid(SQ[:, j % 2, :], TC), AX.X, ALU.add).then_inc(sem("gn_ss"), 1)

            for j in range(13):
                gi = 12 * gr + j
                if j < 12:
                    tile = 8 * (j // 4) + HG * gr + j % 4
                    dve.wait_ge(*count("gp_copied", gi + 1))
                    if gi >= 2:
                        dve.wait_ge(*count("gc_silu", gi - 1))
                    acc, pb = ACC[:, gi % 2, :], PB[:, gi % 2, :]
                    for tap in range(5):
                        w = half_conv[:, 5 * tile + tap:5 * tile + tap + 1]
                        if tap == 0:
                            dve.tensor_scalar(acc, pb[:, 0:T], w, None, ALU.mult).then_inc(sem("gc_tap"), 1)
                        else:
                            dve.wait_ge(*count("gc_tap", 5 * gi + tap))
                            dve.scalar_tensor_tensor(acc, pb[:, tap:tap + T], w, acc, ALU.mult, ALU.add)\
                                .then_inc(sem("gc_tap"), 1)
                if j >= 1:
                    dve.wait_ge(*count("gc_tanh", gi))
                    dve.scalar_tensor_tensor(RAW[:, j - 1, :], TH[:, (gi - 1) % 2, :], 1.0, ACC[:, (gi - 1) % 2, :],
                                             ALU.add, ALU.mult).then_inc(sem("gc_silu"), 1)
                if 4 <= j < 12:
                    sum_squares(j - 4)
            dve.wait_ge(*count("gn_r", gr + 1))
            dve.tensor_scalar(rnorm[:, 0:4, :], rnorm[:, 0:4, :], P ** -0.5, None, ALU.mult).then_inc(sem("gn_q"), 1)
            dve.wait_ge(*count("gn_q", gr + 1))
            for j in range(8):
                t = grid(TOK[:, j, :], TC)
                dve.tensor_tensor(t, t, spread(rnorm[:, j, :], P), ALU.mult).then_inc(sem("gn_scaled"), 1)

        def group_pool(pool, gr):
            split_pool(pool, ("g", gr, 0))
            split_pool(pool, ("g", gr, 1))
            for j in range(8):
                n = 8 * gr + j
                if j % 2 == 0:
                    split_pool(pool, ("g", gr, j // 2 + 2))
                pool.wait_ge(*count("gt_copied", 12 * gr + j + 1))
                if n >= 2:
                    pool.wait_ge(*count("gn_ss", n - 1))
                pool.tensor_tensor(SQ[:, j % 2, :], TOK[:, j, :], TOK[:, j, :], ALU.mult).then_inc(sem("gn_sq"), 1)

        def head_pe(pe, gr, hl):
            n = HG * gr + hl
            if hl == 0:
                pe.wait_ge(*count("gn_back", 8 * (gr + 1)))
            if n:
                pe.wait_ge(*count("gd_qk", 2 * n))
                pe.wait_ge(*count("gd_pt", 2 * n))
            for b, j in ((0, HG + hl), (1, hl)):
                for c in range(TC):
                    mm = pe.matmul(PS[:, b, block_of(c)], RAW[:, HG + hl, block_of(c)], RAW[:, j, block_of(c)],
                                   start=True, stop=True)
            mm.then_inc(sem("gd_gram"), 1)
            for d in range(2):
                pe.wait_ge(*count("gd_tri", 2 * n + d + 1))
                pe.matmul(PS[:, 2 + 3 * d, :], ones, GT[:, d, :], start=True, stop=True).then_inc(sem("gd_row"), 1)
            inverse_pe(pe, n, INV, [XTD[d][:, hl, :] for d in range(2)])

        def head_act(act, gr, hl):
            n = HG * gr + hl
            for d in range(2):
                act.wait_ge(*count("gd_row", 2 * n + d + 1))
                if n:
                    act.wait_ge(*count("gd_qdec", 2 * n - 2 + d + 1))
                act.activation(EGR[:, d, :], PS[:, 2 + 3 * d, :], ACT.Exp).then_inc(sem("gd_eg"), 1)
            for d in range(2):
                act.wait_ge(*count("gd_diff", 2 * (2 * n + d + 1)))
                act.activation(DE[:, d, :], DE[:, d, :], ACT.Exp).then_inc(sem("gd_decay"), 1)
            inverse_act(act, n, INV)

        def head_dve(dve, gr, hl):
            n, h = HG * gr + hl, HG * gr + hl
            for d in range(2):
                if n:
                    dve.wait_ge(*count("gd_row", 2 * n - 1 + d))
                dve.tensor_tensor(grid(GT[:, d, :], TC), every(upto[d], TC),
                                  Gd[:, :, 8 * d + h:8 * d + h + 1].to_broadcast([P, TC, P]), ALU.mult)\
                    .then_inc(sem("gd_tri"), 1)
            for d in range(2):
                m = 2 * n + d
                dve.wait_ge(*count("gd_eg", m + 1))
                if n:
                    dve.wait_ge(*count("gd_qk", m - 1))
                dve.tensor_tensor(grid(DE[:, d, :], TC), grid(PS[:, 2 + 3 * d, :], TC),
                                  GC[:, d, :, h:h + 1].to_broadcast([P, TC, P]), ALU.subtract).then_inc(sem("gd_diff"), 1)
                dve.wait_ge(*count("gd_diff", 2 * m + 1))
                dve.tensor_scalar(DE[:, d, :], DE[:, d, :], 0.0, None, ALU.min).then_inc(sem("gd_diff"), 1)
            dve.wait_ge(*count("gd_gram", n + 1))
            for d in range(2):
                m = 2 * n + d
                dve.wait_ge(*count("gd_decay", m + 1))
                if n:
                    dve.wait_ge(*count(f"inv_lt{d}", 7 * n))
                dve.tensor_tensor(INV[d]["PT"], PS[:, 0, :], DE[:, d, :], ALU.mult).then_inc(sem("gd_pt"), 1)
            for d in range(2):
                m = 2 * n + d
                dve.wait_ge(*count("gd_mask", m + 1))
                dve.tensor_tensor(QKD[d][:, hl, :], PS[:, 1, :], DE[:, d, :], ALU.mult).then_inc(sem("gd_qk"), 1)
            inverse_dve(dve, n, INV, [XTD[d][:, hl, :] for d in range(2)])

        def head_pool(pool, gr, hl):
            n, h = HG * gr + hl, HG * gr + hl
            for d in range(2):
                m = 2 * n + d
                pool.wait_ge(*count("gd_pt", m + 1))
                t = grid(INV[d]["PT"], TC)
                pool.tensor_tensor(t, t, BETA[:, :, 8 * d + h:8 * d + h + 1].to_broadcast([P, TC, P]), ALU.mult)\
                    .then_inc(sem(f"inv_pt{d}"), 1)
                t = grid(DE[:, d, :], TC)
                pool.tensor_tensor(t, t, every(upto[d], TC), ALU.mult).then_inc(sem("gd_mask"), 1)
            for d in range(2):
                m = 2 * n + d
                pool.wait_ge(*count("gd_eg", m + 1))
                pool.wait_ge(*count("gd_gram", n + 1))
                pool.tensor_tensor(qdec(d, hl), RAW[:, hl, :], EGR[:, d, :], ALU.mult).then_inc(sem("gd_qdec"), 1)
            inverse_pool(pool, n, INV, [lev_f, lev_b])

        def qdec(d, hl):
            return TOK[:, hl, :] if d == 0 else RAW[:, 8 + hl, :]

        def chunk_of(d, s):
            return s if d == 0 else TC - 1 - s

        def heads_col(t, d, c, gr):
            return spread(t[:, d, c, HG * gr:HG * gr + HG], P)

        def beta_col(t, d, c, gr):
            return spread(t[:, c, 8 * d + HG * gr:8 * d + HG * gr + HG], P)

        def scan_pe(pe, gr):
            pe.wait_ge(*count("inv_x0", 13 * HG * (gr + 1)))
            pe.wait_ge(*count("inv_x1", 13 * HG * (gr + 1)))
            pe.wait_ge(*count("gd_qdec", 2 * HG * (gr + 1)))
            pe.wait_ge(*count("gd_qk", 2 * HG * (gr + 1)))
            for s in range(TC):
                for d in range(2):
                    if s == 0:
                        continue
                    c = block_of(chunk_of(d, s))
                    pe.wait_ge(*count(f"sc_state{d}", 3 * gr + s))
                    for h in range(HG):
                        mm = pe.matmul(PS[:, 4 * d, block_of(h)], RAW[:, HG + h, c], SC[d]["S"][:, block_of(h)],
                                       start=True, stop=True)
                    mm.then_inc(sem(f"sc_ks{d}"), 1)
                for d in range(2):
                    c, k = block_of(chunk_of(d, s)), TC * gr + s
                    if s:
                        pe.wait_ge(*count(f"sc_r{d}", 3 * gr + s))
                    if k:
                        pe.wait_ge(*count(f"sc_vn{d}", k))
                    for h in range(HG):
                        rhs = TOK[:, 8 + h, c] if s == 0 else SC[d]["R"][:, block_of(h)]
                        mm = pe.matmul(PS[:, 4 * d + 1, block_of(h)], XTD[d][:, h, c], rhs, start=True, stop=True)
                    mm.then_inc(sem(f"sc_y{d}"), 1)
                for d in range(2):
                    c, k = block_of(chunk_of(d, s)), TC * gr + s
                    pe.wait_ge(*count(f"sc_vn{d}", k + 1))
                    if s:
                        pe.wait_ge(*count(f"sc_first{d}", 2 * gr + min(s, 2)))
                    if k > 2:
                        pe.wait_ge(*count(f"sc_second{d}", 2 * gr + max(s - 2, 0)))
                    for h in range(HG):
                        o = PS[:, 4 * d + 2, block_of(h)]
                        mm = pe.matmul(o, SC[d]["VN"][:, block_of(h)], QKD[d][:, h, c], start=True, stop=(s == 0))
                        if s:
                            mm = pe.matmul(o, SC[d]["S"][:, block_of(h)], qdec(d, h)[:, c], start=False, stop=True)
                    mm.then_inc(sem(f"sc_o{d}"), 1)
                    if s == TC - 1:
                        continue
                    pe.wait_ge(*count(f"sc_kdv{d}", 3 * gr + s + 1))
                    for h in range(HG):
                        mm = pe.matmul(PS[:, 4 * d + 3, block_of(h)], TOK[:, HG + h, c], SC[d]["KDV"][:, block_of(h)],
                                       start=True, stop=True)
                    mm.then_inc(sem(f"sc_su{d}"), 1)

        def scan_act(act, gr):
            split_act(act, ("g", 1, 0) if gr == 0 else ("z", 0))
            for s in range(2):
                for d in range(2):
                    act.wait_ge(*count(f"sc_o{d}", TC * gr + s + 1))
                    act.activation(OG[:, HG * gr:HG * gr + HG, block_of(chunk_of(d, s))],
                                   grid(PS[:, 4 * d + 2, :], HG), ACT.Copy).then_inc(sem(f"sc_first{d}"), 1)

        def scan_dve(dve, gr):
            for s in range(TC):
                for d in range(2):
                    if s == 0:
                        continue
                    c, q = chunk_of(d, s), SC[d]
                    dve.wait_ge(*count(f"sc_ks{d}", 3 * gr + s))
                    dve.tensor_tensor(grid(q["R"], HG), grid(PS[:, 4 * d, :], HG), heads_col(NEG_EG, d, c, gr), ALU.mult)\
                        .then_inc(sem(f"sc_t{d}"), 1)
                    dve.wait_ge(*count(f"sc_t{d}", 3 * gr + s))
                    dve.tensor_tensor(grid(q["R"], HG), grid(q["R"], HG), TOK[:, 8:12, block_of(c)], ALU.add)\
                        .then_inc(sem(f"sc_r{d}"), 1)
                for d in range(2):
                    c, q, k = chunk_of(d, s), SC[d], TC * gr + s
                    dve.wait_ge(*count(f"sc_y{d}", k + 1))
                    dve.tensor_tensor(grid(q["VN"], HG), grid(PS[:, 4 * d + 1, :], HG), beta_col(BETA, d, c, gr), ALU.mult)\
                        .then_inc(sem(f"sc_vn{d}"), 1)
                    if s < TC - 1:
                        dve.wait_ge(*count(f"sc_vn{d}", k + 1))
                        dve.tensor_tensor(grid(q["KDV"], HG), grid(q["VN"], HG), heads_col(KD, d, c, gr), ALU.mult)\
                            .then_inc(sem(f"sc_kdv{d}"), 1)
                for d in range(2):
                    c, q, k = chunk_of(d, s), SC[d], TC * gr + s
                    if s == TC - 1:
                        continue
                    dve.wait_ge(*count(f"sc_su{d}", 3 * gr + s + 1))
                    if s == 0:
                        dve.tensor_copy(q["S"], PS[:, 4 * d + 3, :]).then_inc(sem(f"sc_state{d}"), 1)
                        continue
                    dve.tensor_tensor(grid(q["S"], HG), grid(q["S"], HG), beta_col(GL, d, c, gr), ALU.mult)\
                        .then_inc(sem(f"sc_faded{d}"), 1)
                    dve.wait_ge(*count(f"sc_faded{d}", 2 * gr + s))
                    dve.tensor_tensor(q["S"], q["S"], PS[:, 4 * d + 3, :], ALU.add).then_inc(sem(f"sc_state{d}"), 1)
                for d in range(2):
                    if s < 2:
                        continue
                    c = chunk_of(d, s)
                    dve.wait_ge(*count(f"sc_o{d}", TC * gr + s + 1))
                    dve.wait_ge(*count(f"sc_first{1 - d}", 2 * gr + 2))
                    o = OG[:, HG * gr:HG * gr + HG, block_of(c)]
                    dve.tensor_tensor(o, o, grid(PS[:, 4 * d + 2, :], HG), ALU.add).then_inc(sem(f"sc_second{d}"), 1)

        ZS = at(G0 + 512, 2, T)
        ZT = at(G0 + 1536, 2, T)
        ZSQ = at(G0 + 2560, 2, T)
        ZL = at(G0 + 3584, 2, T)
        ZR = at(G0 + 4608, 2, T)

        def gate_pe(pe):
            def norms(h):
                pe.wait_ge(*count("zn_sq", h + 1))
                if h >= 2:
                    pe.wait_ge(*count("zn_ln", h - 1))
                pe.matmul(PS[:, 2 + h % 2, :], ones, ZSQ[:, h % 2, :], start=True, stop=True).then_inc(sem("zn_sum"), 1)

            for d in range(2):
                pe.wait_ge(*count(f"sc_second{d}", 4))
                pe.wait_ge(*count(f"sc_state{d}", 6))
            for h in range(GH):
                if h % 2 == 0:
                    if h == 0:
                        pe.wait_ge(*count("low_back", 64))
                    await_split(pe, ("z", h // 2))
                if h >= 2:
                    pe.wait_ge(*count("z_silu", h - 1))
                split_tile(pe, PS[:, h % 2, :], parts_of(("z", h // 2)), P * (h % 2), HTL).then_inc(sem("z_proj"), 1)
                for k in ((0, 1, 2, 3), (4, 5, 6, 7)):
                    if h == k[0] // 4:
                        for j in k:
                            norms(j)

        def gate_act(act):
            for d in range(2):
                act.wait_ge(*count(f"sc_second{d}", 4))
            for h in range(GH):
                if h == 4:
                    split_act(act, ("z", 1))
                if h >= 2:
                    act.wait_ge(*count("zn_sum", h - 1))
                act.activation(ZSQ[:, h % 2, :], OG[:, h, :], ACT.Square).then_inc(sem("zn_sq"), 1)
                act.wait_ge(*count("zn_sum", h + 1))
                act.activation(ZL[:, h % 2, :], PS[:, 2 + h % 2, :], ACT.Ln, bias=eps, scale=1.0 / P)\
                    .then_inc(sem("zn_ln"), 1)
                act.wait_ge(*count("zn_ln", h + 1))
                if h >= 2:
                    act.wait_ge(*count("zn_norm", h - 1))
                act.activation(ZR[:, h % 2, :], ZL[:, h % 2, :], ACT.Exp, scale=-0.5).then_inc(sem("zn_r"), 1)
            for h in range(GH):
                if h % 2 == 0 and h:
                    split_act(act, after(("z", h // 2)) or ("m", 0, 2))
                act.wait_ge(*count("z_proj", h + 1))
                if h >= 2:
                    act.wait_ge(*count("z_silu", h - 1))
                act.activation(ZT[:, h % 2, :], PS[:, h % 2, :], ACT.Tanh, scale=0.5).then_inc(sem("z_tanh"), 1)

        def gate_dve(dve):
            for h in range(GH):
                dve.wait_ge(*count("zn_r", h + 1))
                dve.tensor_tensor(OG[:, h, :], OG[:, h, :], ZR[:, h % 2, :], ALU.mult).then_inc(sem("zn_norm"), 1)
            for h in range(GH):
                dve.wait_ge(*count("z_tanh", h + 1))
                dve.scalar_tensor_tensor(ZS[:, h % 2, :], ZT[:, h % 2, :], 1.0, PS[:, h % 2, :], ALU.add, ALU.mult)\
                    .then_inc(sem("z_silu"), 1)
                dve.wait_ge(*count("z_silu", h + 1))
                dve.wait_ge(*count("zn_norm", h + 1))
                dve.scalar_tensor_tensor(OG[:, h, :], ZS[:, h % 2, :], gdn_half, OG[:, h, :], ALU.mult, ALU.mult)\
                    .then_inc(sem("z_og"), 1)

        OT2 = at(M_DYN, AH, T)
        MT = at(M_DYN + 4096, DC, T)
        MG_T = at(M_DYN + 8192, 4, T)
        MG_N = at(M_DYN + 10240, 2, T)

        def merge_pe(pe):
            for k in range(4):
                for m in range(4):
                    (await_slot if m < 2 else await_split)(pe, ("m", k, m))
                    if k == 0 and m == 0:
                        pe.wait_ge(*count("ot_back", 16))
                        pe.wait_ge(*count("z_og", GH))
                        pe.wait_ge(*count("z_silu", GH))
                    if k:
                        pe.wait_ge(*count("mg_done", 4 * (k - 1) + (2, 4, 2, 4)[m]))
                    for j in range(2):
                        out = PS[:, 2 * m + j, :]
                        if m < 2:
                            mm = feature_tile(pe, out, slot_of(("m", k, m)), P * j, (OT2, OG)[m])
                        else:
                            mm = split_tile(pe, out, parts_of(("m", k, m)), P * j, HTL)
                        mm.then_inc(sem("mg_proj"), 1)
            pe.wait_ge(*count("mg_sum", DC))
            pe.wait_ge(*count("mg_done", 16))
            for p in range(16):
                j, tc = p // 4, p % 4
                if tc == 0:
                    await_slot(pe, ("o", j))
                if p >= 8:
                    pe.wait_ge(*count("x1_done", p - 7))
                token_tile(pe, PS[:, p % 8, 0:256], slot_of(("o", j)), MT, tc).then_inc(sem("out_proj"), 1)

        def merge_act(act):
            for k in range(4):
                if k:
                    split_act(act, ("m", k, 2))
                split_act(act, ("m", k, 3))
                for m in (2, 3):
                    for j in range(2):
                        act.wait_ge(*count("mg_proj", 8 * k + 2 * m + j + 1))
                        if k:
                            act.wait_ge(*count("mg_done", 4 * (k - 1) + 2 * (m - 2) + j + 1))
                        act.activation(MG_T[:, 2 * (m - 2) + j, :], PS[:, 2 * m + j, :], ACT.Tanh, scale=0.5)\
                            .then_inc(sem("mg_tanh"), 1)

        def merge_dve(dve):
            for k in range(4):
                for m in range(2):
                    for j in range(2):
                        dve.wait_ge(*count("mg_tanh", 4 * k + 2 * m + j + 1))
                        dst = MT[:, 2 * k + j, :] if m == 0 else MG_N[:, j, :]
                        if m and k:
                            dve.wait_ge(*count("mg_sum", 2 * k - 1 + j))
                        dve.scalar_tensor_tensor(dst, MG_T[:, 2 * m + j, :], 1.0, PS[:, 2 * m + j, :], ALU.add, ALU.mult)\
                            .then_inc(sem("mg_done"), 1)
                for j in range(2):
                    dve.wait_ge(*count("mg_done", 4 * k + 3 + j))
                    dve.tensor_tensor(MT[:, 2 * k + j, :], MT[:, 2 * k + j, :], MG_N[:, j, :], ALU.add)\
                        .then_inc(sem("mg_sum"), 1)
            dve.wait_ge(*count("x_back", 16))
            for p in range(16):
                j, tc = p // 4, p % 4
                dve.wait_ge(*count("out_proj", p + 1))
                xs = X[:, tc, 256 * j:256 * (j + 1)]
                dve.scalar_tensor_tensor(xs, PS[:, p % 8, 0:256], 0.5, xs, ALU.mult, ALU.add)\
                    .then_inc(sem("x1_done"), 1)

        def GDN_PE(pe):
            pe.wait_ge(*count("an_ot", AH))
            for gr in range(2):
                group_pe(pe, gr)
                for hl in range(HG):
                    head_pe(pe, gr, hl)
                scan_pe(pe, gr)
            gate_pe(pe)
            merge_pe(pe)

        def GDN_ACT(act):
            act.wait_ge(*count("ot_out", 16))
            for gr in range(2):
                if gr:
                    act.wait_ge(*count("sc_o0", TC))
                    act.wait_ge(*count("sc_o1", TC))
                group_act(act, gr)
                for hl in range(HG):
                    head_act(act, gr, hl)
                scan_act(act, gr)
            gate_act(act)
            merge_act(act)

        def GDN_DVE(dve):
            dve.wait_ge(*count("ot_out", 16))
            dve.memset(PB, 0.0).then_inc(sem("pads"), 1)
            for gr in range(2):
                if gr:
                    dve.wait_ge(*count("sc_o0", TC))
                    dve.wait_ge(*count("sc_o1", TC))
                group_dve(dve, gr)
                for hl in range(HG):
                    head_dve(dve, gr, hl)
                scan_dve(dve, gr)
            gate_dve(dve)
            merge_dve(dve)

        def low_parts_back(pool, gr):
            pool.wait_ge(*count("low_out", 32))
            pool.wait_ge(*count("sc_o0", TC * (gr + 1)))
            pool.wait_ge(*count("sc_o1", TC * (gr + 1)))
            for s in range(2):
                pool.dma_start(r32(half_at(M_DYN + 16384, s)), htl_dram[:, s * SLOT:(s + 1) * SLOT])\
                    .then_inc(sem("low_back"), 16)

        def GDN_POOL(pool):
            for gr in range(2):
                if gr:
                    low_parts_back(pool, 0)
                group_pool(pool, gr)
                for hl in range(HG):
                    head_pool(pool, gr, hl)


        def gate_pool(pool):
            low_parts_back(pool, 1)
            for j in range(4):
                split_pool(pool, ("z", j))
            for k in range(4):
                for m in (2, 3):
                    split_pool(pool, ("m", k, m))
        M_MOE = M_RING
        MSLOT = DC * 512
        MSLOTS = 6
        moe_ring = [M_MOE + s * MSLOT for s in (5, 2, 1, 4, 0, 3)]
        FREE = ((("z_og", GH), ("z_silu", GH)), (("mg_proj", 26),), (("mg_proj", 32),),
                (("mg_done", 16), ("mg_sum", DC)), (("out_proj", 12),), (("out_proj", 16),))
        E0 = M_MOE + MSLOTS * MSLOT
        XE = at(E0, DC, P)
        HE = [at(E0 + 1024 + 1024 * e, FF // P, CAP) for e in range(2)]
        YE = at(E0 + 3072, D)
        SEL = at(E0 + 4096, TC, P)
        SELR = at(E0 + 4608, TC, P)
        SELW = at(E0 + 5120, TC, P)
        SELT = at(E0 + 5632, T)
        ETH = at(E0 + 6144, T)
        ES = at(E0 + 6656, T)
        SELW2 = at(M_DYN + 26592, TC, P)
        SELT2 = at(M_DYN + 27104, T)
        HTOK2 = [at(M_DYN + 27616 + T * n, T) for n in range(2)]
        ACCX = at(M_HT, TC, D)
        R0 = E0 + 7168
        w_r = at(R0, DC, NE)
        LOG = at(R0 + 128, TC, NE)
        AFF = at(R0 + 192, TC, NE)
        rmax = at(R0 + 256, TC)
        rsum = at(R0 + 260, TC)
        rrec = at(R0 + 264, TC)
        ATW = at(R0 + 272, 2, T)
        top8 = at(R0 + 1296, 8, 8)
        CUM = at(R0 + 1360, T)
        MASK = at(R0 + 1872, T)
        ONE = at(R0 + 2384, T)
        POS = at(R0 + 2896, NE, TC)
        AFH = at(R0 + 2960, NE, TC)
        POS2 = at(R0 + 3024, 2, TC)
        AFH2 = at(R0 + 3032, 2, TC)
        NORMF = at(M_DYN + 28672, D)
        assert R0 + 3040 <= M_DYN + 26592
        PAIRS = NE // 2

        def chunk_kind(k):
            e, k = divmod(k, 12)
            if k < 8:
                return ("gate", "up")[k % 4 // 2], e, 2 * (k // 4) + k % 2
            return "down", e, k - 8

        wg_v = a["w_gate"][0].rearrange("(i e) (dc p) n -> i e p dc n", e=2, p=P)
        wu_v = a["w_up"][0].rearrange("(i e) (dc p) n -> i e p dc n", e=2, p=P)
        wd_v = a["w_down"][0].rearrange("(i e) (f p) n -> i e p f n", e=2, p=P)

        def moe_load(eng, i, k):
            kind, e, q = chunk_kind(k)
            o = moe_ring[k % MSLOTS]
            if kind == "down":
                src, dst = wd_v[i, e, :, 4 * q:4 * q + 4, :], at(o, 4, D)
            else:
                src, dst = (wg_v if kind == "gate" else wu_v)[i, e, :, :, 512 * q:512 * q + 512], at(o, DC, 512)
            if not isinstance(i, int):
                src = src.rearrange("a p x n -> (a p) x n")
            eng.dma_start(dst, src).then_inc(sem(f"mo_in{k % MSLOTS}"), 16)

        def moe_loads(eng):
            for k in range(24):
                if k < MSLOTS:
                    for name, value in FREE[k]:
                        eng.wait_ge(*count(name, value))
                else:
                    eng.wait_ge(*count("mo_used", k - MSLOTS + 1))
                moe_load(eng, 0, k)
            with eng.Fori(1, PAIRS) as i:
                for k in range(24):
                    eng.wait_ge(*count("mo_used", i * 24 + (k - MSLOTS + 1)))
                    moe_load(eng, bass.ds(i, 1), k)

        def moe_sp(sp):
            sp.wait_ge(*count("z_og", GH))
            sp.wait_ge(*count("ext_out", 16))
            sp.dma_start(w_r, a["w_router"][0].rearrange("(dc p) n -> p dc n", p=P)).then_inc(sem("router_in"), 16)
            sp.dma_start(NORMF, a["rows"][0].unsqueeze(0).to_broadcast([P, D])).then_inc(sem("router_in"), 16)
            moe_loads(sp)

        def router_pe(pe):
            pe.wait_ge(*count("x1_done", 16))
            norm_pe(pe, "n2")
            pe.wait_ge(*count("n2_ht", DC))
            pe.wait_ge(*count("router_in", 32))
            for tc in range(TC):
                for dc in range(DC):
                    mm = pe.matmul(PS[:, 2, tc * NE:(tc + 1) * NE], HT[:, dc, tc * P:(tc + 1) * P], w_r[:, dc, :],
                                   start=(dc == 0), stop=(dc == DC - 1))
            mm.then_inc(sem("ro_logits"), 1)
            pe.wait_ge(*count("ro_aff", 1))
            for tc in range(TC):
                mm = pe.transpose(PS[0:NE, 3, tc * P:(tc + 1) * P], AFF[:, tc, :], ident)
            mm.then_inc(sem("ro_turned"), 1)
            pe.wait_ge(*count("ro_slot", 1))
            for tc in range(TC):
                mm = pe.transpose(PS[:, 3, tc * NE:(tc + 1) * NE], CUM[0:NE, tc * P:(tc + 1) * P], ident[0:NE, 0:NE])
            mm.then_inc(sem("ro_turned"), 1)

        def router_act(act):
            norm_act(act, "n2", [("x1_done", 16)], "norm2")
            act.wait_ge(*count("ro_shift", 1))
            act.activation(AFF, LOG, ACT.Exp).then_inc(sem("ro_exp"), 1)

        def router_dve(dve):
            norm_dve(dve, "n2")
            dve.wait_ge(*count("ro_logits", 1))
            lg = grid(PS[:, 2, 0:TC * NE], TC)
            dve.tensor_reduce(rmax, lg, AX.X, ALU.max).then_inc(sem("ro_max"), 1)
            dve.wait_ge(*count("ro_max", 1))
            dve.tensor_tensor(LOG, lg, spread(rmax, NE), ALU.subtract).then_inc(sem("ro_shift"), 1)
            dve.wait_ge(*count("ro_exp", 1))
            dve.tensor_reduce(rsum, AFF, AX.X, ALU.add).then_inc(sem("ro_sum"), 1)
            dve.wait_ge(*count("ro_sum", 1))
            dve.reciprocal(rrec, rsum).then_inc(sem("ro_sum"), 1)
            dve.wait_ge(*count("ro_sum", 2))
            dve.tensor_tensor(AFF, AFF, spread(rrec, NE), ALU.mult).then_inc(sem("ro_aff"), 1)
            for tc in range(TC):
                dve.tensor_copy(ACCX[:, tc, :], X[:, tc, :]).then_inc(sem("mo_start"), 1)
            dve.wait_ge(*count("ro_turned", 1))
            dve.tensor_copy(ATW[0:NE, 0, :], PS[0:NE, 3, :]).then_inc(sem("ro_round"), 1)
            for r in range(CAP // 8):
                dve.wait_ge(*count("ro_round", r + 1))
                dve.max(top8[0:NE, r, :], ATW[0:NE, r % 2, :]).then_inc(sem("ro_top"), 1)
                dve.wait_ge(*count("ro_top", r + 1))
                dve.match_replace(ATW[0:NE, (r + 1) % 2, :], top8[0:NE, r, :], ATW[0:NE, r % 2, :], -1.0)\
                    .then_inc(sem("ro_round"), 1)
            dve.wait_ge(*count("ro_round", CAP // 8 + 1))
            dve.memset(ONE[0:NE, :], 1.0).then_inc(sem("ro_mask"), 1)
            dve.tensor_scalar(MASK[0:NE, :], ATW[0:NE, 0, :], 0.0, None, ALU.is_lt).then_inc(sem("ro_mask"), 1)
            dve.wait_ge(*count("ro_mask", 2))
            dve.tensor_tensor_scan(CUM[0:NE, :], ONE[0:NE, :], MASK[0:NE, :], 0.0, ALU.mult, ALU.add)\
                .then_inc(sem("ro_mask"), 1)
            dve.wait_ge(*count("ro_mask", 3))
            dve.tensor_tensor(CUM[0:NE, :], CUM[0:NE, :], MASK[0:NE, :], ALU.mult).then_inc(sem("ro_mask"), 1)
            dve.wait_ge(*count("ro_mask", 4))
            dve.tensor_scalar(CUM[0:NE, :], CUM[0:NE, :], -1.0, None, ALU.add).then_inc(sem("ro_slot"), 1)
            dve.wait_ge(*count("ro_turned", 2))
            dve.tensor_copy(POS.rearrange("p e t -> p t e"), grid(PS[:, 3, 0:TC * NE], TC)).then_inc(sem("ro_pos"), 1)
            dve.wait_ge(*count("ro_aff", 1))
            dve.tensor_scalar(AFH.rearrange("p e t -> p t e"), AFF, 0.5, None, ALU.mult).then_inc(sem("ro_pos"), 1)
            dve.wait_ge(*count("ro_pos", 2))
            dve.wait_ge(*count("mo_start", TC))

        def experts_pe(pe):
            with pe.Fori(0, PAIRS) as i:
                pe.wait_ge(*count("mo_sel", i * 7 + 3))
                pe.wait_ge(*count("mo_acc", i * 8))
                pe.wait_ge(*count("ro_pos", 1))
                for dc in range(DC):
                    for tc in range(TC):
                        mm = pe.matmul(PS[:, dc // 4, (dc % 4) * P:(dc % 4 + 1) * P], X[:, tc, dc * P:(dc + 1) * P],
                                       SELR[:, tc, :], start=(tc == 0), stop=(tc == TC - 1))
                    if dc % 4 == 3:
                        mm.then_inc(sem("mo_gathered"), 1)
                pe.wait_ge(*count("mo_x", i * 8 + 8))
                for e in range(2):
                    for g in range(2):
                        n = 2 * e + g
                        for m in range(2):
                            k = 12 * e + 4 * g + 2 * m
                            for c in range(2):
                                pe.wait_ge(*count(f"mo_in{(k + c) % MSLOTS}", i * 64 + 16 * ((k + c) // MSLOTS + 1)))
                            if m == 0:
                                pe.wait_ge(*count("mo_h", i * 4 + max(n - 1, 0)))
                            for dc in range(DC):
                                for c in range(2):
                                    mm = pe.matmul(PS[c * CAP:(c + 1) * CAP, 2 + 2 * (n % 2) + m, :],
                                                   XE[:, dc, e * CAP:(e + 1) * CAP],
                                                   at(moe_ring[(k + c) % MSLOTS], DC, 512)[:, dc, :],
                                                   start=(dc == 0), stop=(dc == DC - 1))
                                    if dc == DC - 1:
                                        mm.then_inc(sem("mo_used"), 1)
                    for g in range(2):
                        n = 2 * e + g
                        pe.wait_ge(*count("mo_h", i * 4 + (n + 1)))
                        pe.wait_ge(*count("mo_he", i * 4 + max(n - 1, 0)))
                        if n == 2:
                            pe.wait_ge(*count("mo_selt", i * 2 + 2))
                        for t in range(4):
                            mm = pe.transpose(PS[:, n % 2, t * P:(t + 1) * P], HTOK2[n % 2][:, t * P:(t + 1) * P], ident)
                        mm.then_inc(sem("mo_hturned"), 1)
                    pe.wait_ge(*count("mo_y", i * 4))
                    for f in range(FF // P):
                        k = 12 * e + 8 + f // 4
                        w = at(moe_ring[k % MSLOTS], 4, D)
                        if f % 4 == 0:
                            pe.wait_ge(*count("mo_he", i * 4 + (2 * e + f // 8 + 1)))
                            pe.wait_ge(*count(f"mo_in{k % MSLOTS}", i * 64 + 16 * (k // MSLOTS + 1)))
                        for half in range(2):
                            c = half if e == 0 else 1 - half
                            mm = pe.matmul(PS[c * CAP:(c + 1) * CAP, 6 + half, :], HE[e][:, f, :],
                                           w[:, f % 4, 512 * half:512 * half + 512],
                                           start=(f == 0), stop=(f == FF // P - 1))
                        if f % 4 == 3:
                            mm.then_inc(sem("mo_used"), 1)
                    if e == 0:
                        pe.wait_ge(*count("mo_sel", i * 7 + 7))
                        for b, sel in enumerate((SELW, SELW2)):
                            for tc in range(TC):
                                mm = pe.transpose(PS[:, b, tc * P:(tc + 1) * P], sel[:, tc, :], ident)
                        mm.then_inc(sem("mo_turned"), 1)
                pe.wait_ge(*count("mo_y", i * 4 + 4))
                for m in range(8):
                    if m >= 2:
                        pe.wait_ge(*count("mo_acc", i * 8 + (m - 1)))
                    pe.matmul(PS[:, m % 2, :], (SELT, SELT2)[m % 2][:, (m // 2) * P:(m // 2 + 1) * P],
                              YE[:, 512 * (m % 2):512 * (m % 2) + 512], start=True, stop=True)\
                        .then_inc(sem("mo_scattered"), 1)

        def experts_act(act):
            with act.Fori(0, PAIRS) as i:
                act.wait_ge(*count("mo_used", i * 24))
                for dc in range(DC):
                    act.wait_ge(*count("mo_gathered", i * 2 + (dc // 4 + 1)))
                    act.activation(XE[:, dc, :], PS[:, dc // 4, (dc % 4) * P:(dc % 4 + 1) * P], ACT.Copy,
                                   scale=vec("norm2", dc)).then_inc(sem("mo_x"), 1)
                for e in range(2):
                    for g in range(2):
                        n = 2 * e + g
                        act.wait_ge(*count("mo_used", i * 24 + (12 * e + 4 * g + 2)))
                        act.wait_ge(*count("mo_s", i * 4 + n))
                        act.activation(ETH, PS[:, 2 + 2 * (n % 2), :], ACT.Tanh, scale=0.5).then_inc(sem("mo_tanh"), 1)
                    for g in range(2):
                        n = 2 * e + g
                        act.wait_ge(*count("mo_hturned", i * 4 + (n + 1)))
                        act.activation(HE[e][:, 8 * g:8 * g + 8, :].rearrange("p (h t) c -> p t h c", h=2),
                                       PS[:, n % 2, :].rearrange("p (t h c) -> p t h c", t=4, h=2), ACT.Copy)\
                            .then_inc(sem("mo_he"), 1)
                    act.wait_ge(*count("mo_used", i * 24 + (12 * e + 12)))
                    act.wait_ge(*count("mo_scattered", i * 8))
                    for half in range(2):
                        c = half if e == 0 else 1 - half
                        act.activation(YE[c * CAP:(c + 1) * CAP, 512 * half:512 * half + 512],
                                       PS[c * CAP:(c + 1) * CAP, 6 + half, :], ACT.Copy).then_inc(sem("mo_y"), 1)
                    if e == 0:
                        act.wait_ge(*count("mo_turned", i + 1))
                        act.activation(SELT, PS[:, 0, :], ACT.Copy).then_inc(sem("mo_selt"), 1)
                        act.activation(SELT2, PS[:, 1, :], ACT.Copy).then_inc(sem("mo_selt"), 1)

        def experts_dve(dve):
            with dve.Fori(0, PAIRS) as i:
                dve.wait_ge(*count("mo_sel", i * 7))
                dve.tensor_copy(POS2.rearrange("p e t -> p (e t)"),
                                POS.rearrange("p e t -> p (e t)")[:, bass.ts(i, 2 * TC)]).then_inc(sem("mo_pair"), 1)
                dve.tensor_copy(AFH2.rearrange("p e t -> p (e t)"),
                                AFH.rearrange("p e t -> p (e t)")[:, bass.ts(i, 2 * TC)]).then_inc(sem("mo_pair"), 1)
                dve.wait_ge(*count("mo_pair", i * 2 + 2))
                for e in range(2):
                    dve.tensor_tensor(SEL[:, :, e * CAP:(e + 1) * CAP], spread(POS2[:, e, :], CAP),
                                      every(const("slots"), TC), ALU.is_equal).then_inc(sem("mo_sel"), 1)
                dve.wait_ge(*count("mo_sel", i * 7 + 2))
                dve.wait_ge(*count("mo_gathered", i * 2))
                dve.tensor_tensor(SELR, SEL, spread(rs, P), ALU.mult).then_inc(sem("mo_sel"), 1)
                dve.wait_ge(*count("mo_turned", i))
                for dst, swap in ((SELW, 0), (SELW2, 1)):
                    for e in range(2):
                        o = (e ^ swap) * CAP
                        dve.tensor_tensor(dst[:, :, o:o + CAP], SEL[:, :, e * CAP:(e + 1) * CAP],
                                          spread(AFH2[:, e, :], CAP), ALU.mult).then_inc(sem("mo_sel"), 1)
                for n in range(4):
                    e, g = divmod(n, 2)
                    dve.wait_ge(*count("mo_tanh", i * 4 + (n + 1)))
                    dve.wait_ge(*count("mo_h", i * 4 + n))
                    dve.scalar_tensor_tensor(ES, ETH, 1.0, PS[:, 2 + 2 * (n % 2), :], ALU.add, ALU.mult)\
                        .then_inc(sem("mo_s"), 1)
                    dve.wait_ge(*count("mo_s", i * 4 + (n + 1)))
                    dve.wait_ge(*count("mo_used", i * 24 + (12 * e + 4 * g + 4)))
                    dve.wait_ge(*count("mo_hturned", i * 4 + max(n - 1, 0)))
                    dve.tensor_tensor(HTOK2[n % 2], ES, PS[:, 3 + 2 * (n % 2), :], ALU.mult).then_inc(sem("mo_h"), 1)
                for m in range(8):
                    dve.wait_ge(*count("mo_scattered", i * 8 + (m + 1)))
                    x = ACCX[:, m // 2, 512 * (m % 2):512 * (m % 2) + 512]
                    dve.tensor_tensor(x, x, PS[:, m % 2, :], ALU.add).then_inc(sem("mo_acc"), 1)
                dve.wait_ge(*count("mo_acc", i * 8 + 8))

        def final1_act(act):
            act.wait_ge(*count("mo_acc", 8 * PAIRS))
            for tc in range(TC):
                act.activation(X[:, tc, :], ACCX[:, tc, :], ACT.Square, accum_out=ss[:, tc:tc + 1])\
                    .then_inc(sem("f1_sq"), 1)
            act.wait_ge(*count("f1_sq", TC))
            act.activation(lnv, ss, ACT.Ln, bias=eps, scale=1.0 / D).then_inc(sem("f1_ln"), 1)
            act.wait_ge(*count("f1_ln", 1))
            act.activation(rs, lnv, ACT.Exp, scale=-0.5).then_inc(sem("f1_r"), 1)

        def final1_dve(dve):
            dve.wait_ge(*count("f1_r", 1))
            dve.wait_ge(*count("router_in", 32))
            for tc in range(TC):
                dve.scalar_tensor_tensor(X[:, tc, :], ACCX[:, tc, :], rs[:, tc:tc + 1], NORMF, ALU.mult, ALU.mult)\
                    .then_inc(sem("x2_done"), 1)

        B2 = M_DYN
        loads2 = []
        where2 = {}

        def load2(name, src, dst_shape, done, value):
            where2[name] = len(loads2)
            loads2.append((src, dst_shape, done, value))

        def cols2(w, c, n=256):
            return w[0, :, c:c + n].rearrange("(dc p) n -> p dc n", p=P)

        full, part, rows2 = (DC, 256), (4, 256), (2, D)
        for j in range(4):
            load2(("qk", j), cols2(a["w_in_2"], 256 * j), full, "b_qk", 2 * (j + 1))
        for j in range(2):
            load2(("v", j), cols2(a["w_in_2"], 2 * WA + 256 * j), full, "b_v", TC * (j + 1))
        for j in range(7):
            load2(("r", j), cols2(a["w_in_2"], B2_R + 256 * j), full, "r_proj", 2 * (j + 1))
        for k in range(4):
            for m, (w, c, shape) in enumerate(((a["proj_a_2"], 0, part), (a["proj_b_2"], 0, part),
                                               (a["w_in_2"], B2_GATE, full), (a["w_in_2"], B2_GATE + D, full))):
                load2(("m", k, m), cols2(w, c + 256 * k), shape, "m2_proj", 8 * k + 2 * (m + 1))
        for j in range(4):
            load2(("o", j), cols2(a["w_out_2"], 256 * j), full, "o2_proj", 4 * (j + 1))
        for j in range(16):
            load2(("u", j), cols2(a["w_up_2"], 256 * j), full, "up_proj", 2 * (j + 1))
        for j in range(16):
            load2(("d", j), a["w_down_2"][0, 256 * j:256 * (j + 1), :].rearrange("(f p) n -> p f n", p=P), rows2,
                  "dn_proj", j + 1)

        def slot2(name):
            n = where2[name]
            third = B2 + (16384 if n < where2[("m", 0, 0)] else 22528)
            return at(third if n % SLOTS == 2 else M_RING + (n % SLOTS) * SLOT, *loads2[n][1])

        LOW3 = at(B2 + 22528, DC, T)
        LOW3G = at(B2 + 24576, DC, T)
        LOW4 = at(B2 + 16384, DC, T)
        low2_dram = nc.dram_tensor("low_parts_2", (P, DC * T), F32, kind="Internal").ap()
        splits2 = [n for n in where2 if n[0] in ("qk", "v", "r", "u") or (n[0] == "m" and n[2] >= 2)]
        turn2 = {n: k for k, n in enumerate(splits2)}

        def after2(name):
            k = turn2[name] + 1
            return splits2[k] if k < len(splits2) else None

        def split2_act(act, name):
            k = turn2[name]
            await2(act, name)
            if k >= 2:
                _, _, done, value = loads2[where2[splits2[k - 2]]]
                act.wait_ge(*count(done, value))
            act.activation(r32(WH[k % 2]), slot2(name), ACT.Copy).then_inc(sem("w2_high"), 1)

        def splits2_pool(pool, kinds):
            for name in splits2:
                if name[0] in kinds:
                    k, w = turn2[name], slot2(name)
                    pool.wait_ge(*count("w2_high", k + 1))
                    pool.tensor_tensor(r32(w), w, rounded(WH[k % 2]), ALU.subtract).then_inc(sem("w2_low"), 1)

        def await_split2(pe, name):
            pe.wait_ge(*count("w2_low", turn2[name] + 1))

        def parts2(name):
            return WH[turn2[name] % 2], slot2(name)

        def await2(eng, name):
            n = where2[name]
            eng.wait_ge(*count(f"w2_loaded{n % SLOTS}", 16 * (n // SLOTS + 1)))

        x2_dram = nc.dram_tensor("x_between", (P, TC * D), F32, kind="Internal").ap()
        toe_dram = nc.dram_tensor("bias_rows", (H2, TOE), F32, kind="Internal").ap()

        EXT = at(M_DYN + 28704, TOE)
        REV = at(M_DYN + 28704 + TOE, N_REL)

        def bias_dve(dve):
            dve.wait_ge(*count("rev_in", 16))
            e, r = EXT[0:H2, :], REV[0:H2, :]
            dve.tensor_copy(e[:, 255:575], r).then_inc(sem("ext_set"), 1)
            dve.tensor_copy(e[:, 0:255], r[:, 0:1].to_broadcast([H2, 255])).then_inc(sem("ext_set"), 1)
            dve.tensor_copy(e[:, 575:TOE], r[:, N_REL - 1:N_REL].to_broadcast([H2, TOE - 575])).then_inc(sem("ext_set"), 1)

        QT2 = at(B2, 4, T)
        KT2 = at(B2 + 2048, 4, T)
        V2 = at(B2 + 4096, TC, WA)
        TB = at(B2 + 6144, H2, T)
        TBR = at(B2 + 10240, H2, T)
        SB = at(B2 + 10240, 3, T)
        PT2 = at(B2 + 11776, 2, T)
        YA = at(B2 + 12800, TC, WA)
        nm2 = at(B2 + 14848, 32)
        sm2 = at(B2 + 14880, H2, TC)
        rc2 = at(B2 + 14912, H2, TC)
        VT = at(M_X, TC, WA)
        YAT = at(M_X + 2048, 4, T)
        UNITS2 = H2 * TC

        def bias_pe(pe):
            pe.wait_ge(*count("toe_in", 16))
            for h in range(H2):
                if h >= 4:
                    pe.wait_ge(*count("tb_copied", h - 3))
                pe.matmul(PS[:, 4 + h % 4, :], const("flip"), TBR[:, h, :], start=True, stop=True)\
                    .then_inc(sem("tb_turned"), 1)

        def bias_tiles_dve(dve):
            for h in range(H2):
                dve.wait_ge(*count("tb_turned", h + 1))
                dve.tensor_copy(TB[:, h, :], PS[:, 4 + h % 4, :]).then_inc(sem("tb_copied"), 1)
            dve.wait_ge(*count("tb_copied", H2))
            dve.memset(TB[0:64, :, T - 64:T], -1e30).then_inc(sem("b_masked"), 1)

        def band_pe(pe):
            pe.wait_ge(*count("n3_lo", DC))
            for p in range(8):
                if p % 2 == 0:
                    await_split2(pe, ("qk", p // 2))
                if p >= 2:
                    pe.wait_ge(*count("b_qk_done", p - 1))
                split_tile(pe, PS[:, p % 2, :], parts2(("qk", p // 2)), P * (p % 2), LOW3).then_inc(sem("b_qk"), 1)
            for p in range(8):
                j, tc = p // 4, p % 4
                if tc == 0:
                    await_split2(pe, ("v", j))
                if p < 2:
                    pe.wait_ge(*count("b_qk_done", 8))
                else:
                    pe.wait_ge(*count("b_v_done", p - 1))
                split_token_tile(pe, PS[:, p % 2, 0:256], parts2(("v", j)), LOW3, tc).then_inc(sem("b_v"), 1)
            pe.wait_ge(*count("b_v_done", 8))

            def scores(i):
                h, tc = divmod(i, TC)
                s, n = slice(64 * (h % 2), 64 * (h % 2) + 64), P * (tc + 1)
                if i >= 2:
                    pe.wait_ge(*count("b_biased", i - 1))
                pe.matmul(PS[:, i % 2, 0:n], QT2[s, h // 2, block_of(tc)], KT2[s, h // 2, 0:n], start=True, stop=True)\
                    .then_inc(sem("b_scores"), 1)

            def turn(i):
                h, tc = divmod(i, TC)
                pe.wait_ge(*count("b_exp", i + 1))
                if i >= 2:
                    pe.wait_ge(*count("b_pt", i - 1))
                for kc in range(tc + 1):
                    mm = pe.transpose(PS[:, 2 + i % 2, block_of(kc)], SB[:, i % 3, block_of(kc)], ident)
                mm.then_inc(sem("b_turned"), 1)

            def values(i):
                h, tc = divmod(i, TC)
                pe.wait_ge(*count("b_pt", i + 1))
                if tc == 0 and h >= 2:
                    pe.wait_ge(*count("b_o", h - 1))
                for kc in range(tc + 1):
                    mm = pe.matmul(PS[:, 4 + h % 2, 64 * tc:64 * tc + 64], PT2[:, i % 2, block_of(kc)],
                                   V2[:, kc, 64 * h:64 * h + 64], start=(kc == 0), stop=(kc == tc))
                mm.then_inc(sem("b_pv"), 1)

            for s in range(UNITS2 + 3):
                if s < UNITS2:
                    scores(s)
                if 2 <= s < UNITS2 + 2:
                    turn(s - 2)
                if s >= 3:
                    values(s - 3)
            pe.wait_ge(*count("b_o", H2))
            pe.wait_ge(*count("b_biased", UNITS2))
            for m in range(4):
                if m >= 2:
                    pe.wait_ge(*count("b_yat", m - 1))
                for tc in range(TC):
                    mm = pe.transpose(PS[:, m % 2, block_of(tc)], YA[:, tc, block_of(m)], ident)
                mm.then_inc(sem("b_ya_turned"), 1)

        def band_act(act):
            for p in range(8):
                if p % 2 == 0:
                    split2_act(act, after2(("qk", p // 2)))
                act.wait_ge(*count("b_qk", p + 1))
                dst = (QT2 if p < 4 else KT2)[:, p % 4, :]
                act.activation(dst, PS[:, p % 2, :], ACT.Copy).then_inc(sem("b_qk_done"), 1)
            for p in range(8):
                j, tc = p // 4, p % 4
                if tc == 0:
                    split2_act(act, after2(("v", j)))
                act.wait_ge(*count("b_v", p + 1))
                act.activation(V2[:, tc, 256 * j:256 * (j + 1)], PS[:, p % 2, 0:256], ACT.Copy).then_inc(sem("b_v_done"), 1)
            for s in range(UNITS2 + 2):
                if s < UNITS2:
                    h, tc = divmod(s, TC)
                    act.wait_ge(*count("b_negmax", s + 1))
                    w = SB[:, s % 3, 0:P * (tc + 1)]
                    act.activation(w, w, ACT.Exp, bias=nm2[:, s:s + 1], accum_out=sm2[:, h, tc:tc + 1])\
                        .then_inc(sem("b_exp"), 1)
                if s >= 2:
                    i = s - 2
                    act.wait_ge(*count("b_turned", i + 1))
                    if i >= 2:
                        act.wait_ge(*count("b_pv", i - 1))
                    n = P * (i % TC + 1)
                    act.activation(PT2[:, i % 2, 0:n], PS[:, 2 + i % 2, 0:n], ACT.Copy).then_inc(sem("b_pt"), 1)
            act.wait_ge(*count("x2_kept", 16))
            for m in range(4):
                act.wait_ge(*count("b_ya_turned", m + 1))
                act.activation(YAT[:, m, :], PS[:, m % 2, :], ACT.Copy).then_inc(sem("b_yat"), 1)

        def band_dve(dve):
            dve.wait_ge(*count("b_masked", 1))

            def output(h):
                dve.wait_ge(*count("b_pv", TC * (h + 1)))
                dve.reciprocal(rc2[:, h, :], sm2[:, h, :]).then_inc(sem("b_rc"), 1)
                dve.wait_ge(*count("b_rc", h + 1))
                dve.tensor_tensor(YA[:, :, 64 * h:64 * h + 64], grid(PS[:, 4 + h % 2, 0:256], TC),
                                  spread(rc2[:, h, :], 64), ALU.mult).then_inc(sem("b_o"), 1)

            for s in range(UNITS2):
                h, tc = divmod(s, TC)
                n, o = P * (tc + 1), 384 - P * tc
                dve.wait_ge(*count("b_scores", s + 1))
                if s >= 3:
                    dve.wait_ge(*count("b_turned", s - 2))
                dve.scalar_tensor_tensor(SB[:, s % 3, 0:n], PS[:, s % 2, 0:n], A_SCALE, TB[:, h, o:o + n],
                                         ALU.mult, ALU.add).then_inc(sem("b_biased"), 1)
                dve.wait_ge(*count("b_biased", s + 1))
                dve.tensor_reduce(nm2[:, s:s + 1], SB[:, s % 3, 0:n], AX.X, ALU.max, negate=True)\
                    .then_inc(sem("b_negmax"), 1)
                if s >= 7 and (s - 7) % TC == 0:
                    output((s - 7) // TC)
            output(H2 - 1)

        FR = at(B2, 13, T)
        LW = at(B2 + 7168, 4, T)
        AG = at(B2 + 9216, 4, T)
        TM = at(B2 + 11264, 8, T)
        AR = [at(B2 + 15360 + 1024 * m, TC, 2, P) for m in range(4)]
        BH = at(B2 + 19456, 4, T)
        KH = at(B2 + 21504, 4, T)
        BT = at(B2 + 23552, TC, WA)
        KTK = at(B2 + 25600, TC, WA)
        SIG = at(B2 + 27648, T)
        PADR = at(B2 + 19456, 2, T + 2)
        W2 = at(B2 + 21504, WA)
        A2 = W2
        G2 = at(B2 + 28160, WA)
        small_at[0] = scratch_at
        s_w0h, s_a0h, s_gbh = small(4), small(4), small(16)
        s_ka1 = small(4)
        s_c30 = small(1)
        cmid, cend, e_mid, e_end, e_rest = (small(4, TC) for _ in range(5))
        bon = small(TC, H2)

        def frame(t):
            return FR[:, t, :] if t < 13 else SIG

        def shift_pe(pe):
            pe.wait_ge(*count("b_yat", 4))
            for t in range(14):
                if t % 2 == 0:
                    await_split2(pe, ("r", t // 2))
                if t >= 2:
                    pe.wait_ge(*count("r_copied", t - 1))
                split_tile(pe, PS[:, t % 2, :], parts2(("r", t // 2)), P * (t % 2), LOW3).then_inc(sem("r_proj"), 1)
            pe.wait_ge(*count("lora_in", 32))
            pe.wait_ge(*count("r_copied", 14))
            pe.wait_ge(*count("r_lora", 1))
            for m in range(4):
                if m >= 2:
                    pe.wait_ge(*count("r_gates", 2 * m - 3))
                pe.matmul(PS[:, m % 2, :], W2[0:64, block_of(m)], FR[0:64, 12, :], start=True, stop=True)\
                    .then_inc(sem("r_low"), 1)
                if m >= 2:
                    pe.wait_ge(*count("r_gates", 2 * m - 2))
                pe.matmul(PS[:, 2 + m % 2, :], A2[64:128, block_of(m)], FR[64:128, 12, :], start=True, stop=True)\
                    .then_inc(sem("r_low"), 1)

        def shift_act(act):
            for t in range(14):
                if t % 2 == 0 and t < 12:
                    split2_act(act, ("r", t // 2 + 1))
                act.wait_ge(*count("r_proj", t + 1))
                act.wait_ge(*count("r_pads", 1))
                if t >= 2:
                    act.wait_ge(*count("r_shift", t - 1))
                act.activation(PADR[:, t % 2, 1:1 + T], PS[:, t % 2, :], ACT.Copy).then_inc(sem("r_copied"), 1)
            act.wait_ge(*count("r_shift", 14))
            act.activation(FR[0:64, 12, :], FR[0:64, 12, :], ACT.Tanh).then_inc(sem("r_lora"), 1)
            act.activation(SIG, SIG, ACT.Tanh, scale=0.5).then_inc(sem("r_lora"), 1)
            act.wait_ge(*count("r_halves", 5))
            for m in range(4):
                for w, (dst, bias) in enumerate(((LW, s_w0h), (AG, s_a0h))):
                    act.wait_ge(*count("r_low", 2 * m + w + 1))
                    act.activation(dst[:, m, :], PS[:, 2 * w + m % 2, :], ACT.Tanh, bias=bias[:, m:m + 1], scale=0.5)\
                        .then_inc(sem("r_gates"), 1)

        def shift_dve(dve):
            dve.wait_ge(*count("b_yat", 4))
            dve.memset(PADR, 0.0).then_inc(sem("r_pads"), 1)
            dve.tensor_scalar(s_w0h, vec("w0", 0, 4), 0.5, None, ALU.mult).then_inc(sem("r_halves"), 1)
            dve.tensor_scalar(s_a0h, vec("a0", 0, 4), 0.5, None, ALU.mult).then_inc(sem("r_halves"), 1)
            dve.tensor_scalar(s_gbh, vec("gate_bias", 0, 16), 0.5, None, ALU.mult).then_inc(sem("r_halves"), 1)
            dve.tensor_scalar(s_ka1, vec("k_a", 0, 4), -1.0, 1.0, ALU.mult, ALU.add).then_inc(sem("r_halves"), 1)
            dve.memset(s_c30, 15 * math.log(2.0)).then_inc(sem("r_halves"), 1)
            for t in range(14):
                dve.wait_ge(*count("r_copied", t + 1))
                pad, f = PADR[:, t % 2, :], frame(t)
                dve.tensor_tensor(f, pad[:, 0:T], pad[:, 1:1 + T], ALU.subtract).then_inc(sem("r_diff"), 1)
                dve.wait_ge(*count("r_diff", t + 1))
                dve.scalar_tensor_tensor(f, f, vec("mu", t), pad[:, 1:1 + T], ALU.mult, ALU.add).then_inc(sem("r_shift"), 1)
            dve.wait_ge(*count("r_lora", 2))
            dve.tensor_scalar(SIG, SIG, 0.5, 0.5, ALU.mult, ALU.add).then_inc(sem("r_sig"), 1)
            for m in range(4):
                dve.wait_ge(*count("r_gates", 2 * m + 2))
                dve.tensor_scalar(LW[:, m, :], LW[:, m, :], -0.5 * DECAY_MAX, -0.5 * DECAY_MAX, ALU.mult, ALU.add)\
                    .then_inc(sem("r_sig"), 1)
                dve.tensor_scalar(AG[:, m, :], AG[:, m, :], 0.5, 0.5, ALU.mult, ALU.add).then_inc(sem("r_sig"), 1)

        def tiles_pe(pe):
            for m in range(4):
                pe.wait_ge(*count("t_sq", m + 1))
                if m:
                    pe.wait_ge(*count("t_max", m))
                else:
                    pe.wait_ge(*count("r_gates", 8))
                pe.matmul(PS[:, 4, :], const("heads2"), TM[:, 2, :], start=True, stop=True).then_inc(sem("t_sum"), 1)
                pe.wait_ge(*count("t_bonus", m + 1))
                for tc in range(TC):
                    mm = pe.matmul(PS[:, 5, tc * 8 + 2 * m:tc * 8 + 2 * m + 2], TM[:, 7, block_of(tc)], const("pair"),
                                   start=True, stop=True)
                mm.then_inc(sem("t_bonus_sum"), 1)
                pe.wait_ge(*count("t_hats", 2 * (m + 1)))
                for w, src in enumerate((BH[:, m, :], KH[:, m, :], FR[:, 8 + m, :])):
                    n = 3 * m + w
                    if n >= 2:
                        pe.wait_ge(*count("t_tok", n - 1))
                    for tc in range(TC):
                        mm = pe.transpose(PS[:, 6 + n % 2, block_of(tc)], src[:, block_of(tc)], ident)
                    mm.then_inc(sem("t_turned"), 1)

        def tiles_act(act):
            for m in range(4):
                act.wait_ge(*count("t_kk", m + 1))
                if m:
                    act.wait_ge(*count("t_norm", m))
                act.activation(TM[:, 2, :], TM[:, 1, :], ACT.Square).then_inc(sem("t_sq"), 1)
                act.wait_ge(*count("t_max", m + 1))
                act.activation(TM[:, 2, :], TM[:, 2, :], ACT.Ln, scale=2.0 ** 30).then_inc(sem("t_ln"), 1)
                act.wait_ge(*count("t_ln", m + 1))
                act.activation(TM[:, 2, :], TM[:, 2, :], ACT.Exp, scale=-0.5, bias=s_c30).then_inc(sem("t_rn"), 1)
                act.wait_ge(*count("t_cs", 2 * (m + 1)))
                if m:
                    act.wait_ge(*count("t_hats", 2 * m))
                    act.wait_ge(*count("t_ar", 2 * m))
                act.activation(TM[:, 3, :], TM[:, 0, :], ACT.Exp).then_inc(sem("t_exps"), 1)
                act.activation(TM[:, 5, :], TM[:, 0, :], ACT.Exp, scale=-1.0).then_inc(sem("t_exps"), 1)
                act.activation(TM[:, 4, :], TM[:, 4, :], ACT.Exp).then_inc(sem("t_exps"), 1)
                for w, dst in enumerate((BT, KTK, VT)):
                    act.wait_ge(*count("t_turned", 3 * m + w + 1))
                    act.activation(dst[:, :, block_of(m)], grid(PS[:, 6 + (3 * m + w) % 2, :], TC), ACT.Copy)\
                        .then_inc(sem("t_tok"), 1)
            act.wait_ge(*count("t_ends", 12))
            act.activation(e_mid, cmid, ACT.Exp).then_inc(sem("t_ends_exp"), 1)
            act.activation(e_end, cend, ACT.Exp).then_inc(sem("t_ends_exp"), 1)
            act.activation(e_rest, e_rest, ACT.Exp).then_inc(sem("t_ends_exp"), 1)

        def tiles_dve(dve):
            dve.wait_ge(*count("r_sig", 9))
            for m in range(4):
                C, r, k = TM[:, 0, :], FR[:, m, :], FR[:, 4 + m, :]
                if m:
                    dve.wait_ge(*count("t_exps", 3 * m))
                    dve.wait_ge(*count("t_bonus_sum", m))
                    dve.wait_ge(*count("t_hats", 2 * m))
                dve.tensor_tensor_scan(C, const("reset"), LW[:, m, :], 0.0, ALU.mult, ALU.add).then_inc(sem("t_cum"), 1)
                if m:
                    dve.wait_ge(*count("t_ar", 2 * m))
                dve.tensor_scalar(TM[:, 1, :], k, vec("k_k", m), None, ALU.mult).then_inc(sem("t_kk"), 1)
                dve.tensor_scalar(TM[:, 6, :], AG[:, m, :], vec("k_a", m), s_ka1[:, m:m + 1], ALU.mult, ALU.add)\
                    .then_inc(sem("t_kp"), 1)
                dve.wait_ge(*count("t_kp", 2 * m + 1))
                dve.tensor_tensor(TM[:, 6, :], TM[:, 6, :], k, ALU.mult).then_inc(sem("t_kp"), 1)
                dve.wait_ge(*count("t_cum", m + 1))
                Cg = grid(C, TC)
                dve.tensor_copy(cmid[:, m, :], Cg[:, :, 63]).then_inc(sem("t_ends"), 1)
                dve.tensor_copy(cend[:, m, :], Cg[:, :, P - 1]).then_inc(sem("t_ends"), 1)
                dve.wait_ge(*count("t_ends", 3 * m + 2))
                dve.tensor_tensor(e_rest[:, m, :], cend[:, m, :], cmid[:, m, :], ALU.subtract).then_inc(sem("t_ends"), 1)
                dve.wait_ge(*count("t_ends", 3 * m + 3))
                dve.tensor_tensor(Cg, Cg, spread(cmid[:, m, :], P), ALU.subtract).then_inc(sem("t_cs"), 1)
                dve.wait_ge(*count("t_cs", 2 * m + 1))
                dve.tensor_tensor(TM[:, 4, :], C, LW[:, m, :], ALU.subtract).then_inc(sem("t_cs"), 1)
                dve.wait_ge(*count("t_kp", 2 * m + 2))
                dve.scalar_tensor_tensor(TM[:, 7, :], r, vec("r_k", m), TM[:, 6, :], ALU.mult, ALU.mult)\
                    .then_inc(sem("t_bonus"), 1)
                dve.wait_ge(*count("t_sum", m + 1))
                dve.tensor_scalar(TM[:, 2, :], PS[:, 4, :], 1e-24, None, ALU.max).then_inc(sem("t_max"), 1)
                dve.wait_ge(*count("t_rn", m + 1))
                dve.tensor_tensor(TM[:, 1, :], TM[:, 1, :], TM[:, 2, :], ALU.mult).then_inc(sem("t_norm"), 1)
                dve.wait_ge(*count("t_exps", 3 * (m + 1)))
                dve.wait_ge(*count("t_norm", m + 1))
                dve.tensor_tensor(AR[m][:, :, 0, :], grid(TM[:, 1, :], TC), grid(TM[:, 4, :], TC), ALU.mult)\
                    .then_inc(sem("t_ar"), 1)
                dve.tensor_tensor(AR[m][:, :, 1, :], grid(r, TC), grid(TM[:, 3, :], TC), ALU.mult)\
                    .then_inc(sem("t_ar"), 1)
                dve.tensor_tensor(BH[:, m, :], TM[:, 1, :], AG[:, m, :], ALU.mult).then_inc(sem("t_b"), 1)
                dve.wait_ge(*count("t_b", m + 1))
                dve.tensor_tensor(BH[:, m, :], BH[:, m, :], TM[:, 5, :], ALU.mult).then_inc(sem("t_hats"), 1)
                dve.tensor_tensor(KH[:, m, :], TM[:, 6, :], TM[:, 5, :], ALU.mult).then_inc(sem("t_hats"), 1)
            dve.wait_ge(*count("t_bonus_sum", 4))
            dve.tensor_copy(bon, grid(PS[:, 5, 0:TC * H2], TC)).then_inc(sem("t_bon"), 1)

        XT2 = at(B2, HG, T)
        SCO = [at(B2 + 2048 + 2048 * h, 4, T) for h in range(HG)]
        YTOK = at(B2 + 13312, TC, WA)
        INV2 = [dict(X=at(B2 + 10240 + 1536 * d, T), U=at(B2 + 10752 + 1536 * d, T), LT=at(B2 + 11264 + 1536 * d, T))
                for d in range(2)]
        SP_ = at(B2 + 28672, 4, 64)
        SA_ = at(B2 + 28928, 256)
        HS_ = small(2, 64)
        HH_ = small(2, 64)
        HT_ = small(2, 64)

        def lanes2(m):
            return [dict(INV2[d], PT=SCO[2 * (m % 2) + d][:, 0, :]) for d in range(2)]

        def units_pe(pe, m):
            if m == 0:
                pe.wait_ge(*count("t_bon", 1))
                pe.wait_ge(*count("t_tok", 12))
                pe.wait_ge(*count("t_hats", 8))
            for tc in range(TC):
                for d in range(2):
                    n = 8 * m + 2 * tc + d
                    s = slice(64 * d, 64 * d + 64)
                    if n >= 2:
                        pe.wait_ge(*count("u_masked", n - 1))
                    rhs = AR[m][s, tc, :, :].rearrange("p a b -> p (a b)")
                    pe.matmul(PS[:, d, 0:256], BH[s, m, block_of(tc)], rhs, start=True, stop=True)
                    pe.matmul(PS[:, d, 256:512], KH[s, m, block_of(tc)], rhs, start=True, stop=True)\
                        .then_inc(sem("u_scores"), 1)
            inverse_pe(pe, GH + m, lanes2(m), [XT2[:, 2 * (m % 2) + d, :] for d in range(2)])

        def units_dve(dve, m):
            if m == 0:
                dve.wait_ge(*count("t_tok", 12))
                dve.wait_ge(*count("t_ends_exp", 3))
            if m == 2:
                dve.wait_ge(*count("s_y", TC))
            for tc in range(TC):
                for d in range(2):
                    n = 8 * m + 2 * tc + d
                    dve.wait_ge(*count("u_scores", n + 1))
                    dve.tensor_tensor(SCO[2 * (m % 2) + d][:, :, block_of(tc)], grid(PS[:, d, :], 4),
                                      grid(const("mask4"), 4), ALU.mult).then_inc(sem("u_masked"), 1)
            inverse_dve(dve, GH + m, lanes2(m), [XT2[:, 2 * (m % 2) + d, :] for d in range(2)])

        def units_pool(pool, m):
            pool.wait_ge(*count("u_masked", 8 * (m + 1)))
            inverse_pool(pool, GH + m, lanes2(m), [lev_f, lev_f])

        def state_pe(pe, hf):
            pe.wait_ge(*count("inv_x0", 13 * (GH + 2 * hf + 2)))
            pe.wait_ge(*count("inv_x1", 13 * (GH + 2 * hf + 2)))
            heads = [(h4, 2 * hf + h4 // 2, h4 % 2) for h4 in range(HG)]
            for c in range(TC):
                k = TC * hf + c
                if c:
                    pe.wait_ge(*count("s_scaled", 3 * hf + c))
                for h4, m, d in heads:
                    s, h, o = slice(64 * d, 64 * d + 64), 2 * m + d, PS[:, d, 64 * (m % 2):64 * (m % 2) + 64]
                    mm = pe.matmul(o, SCO[h4][:, 2, block_of(c)], VT[:, c, 64 * h:64 * h + 64], start=True, stop=(c == 0))
                    if c:
                        mm = pe.matmul(o, AR[m][s, c, 0, :], HS_[s, m % 2, :], start=False, stop=True)
                mm.then_inc(sem("s_rhs"), 1)
                pe.wait_ge(*count("s_rhs_copied", k + 1))
                for h4, m, d in heads:
                    mm = pe.matmul(PS[:, 4, 64 * h4:64 * h4 + 64], XT2[:, h4, block_of(c)],
                                   SP_[:, 2 * d + m % 2, :], start=True, stop=True)
                mm.then_inc(sem("s_sa"), 1)
                pe.wait_ge(*count("s_sa_copied", k + 1))
                if k:
                    pe.wait_ge(*count("s_y", k))
                for h4, m, d in heads:
                    if c == TC - 1:
                        break
                    h, o = 2 * m + d, PS[64 * d:64 * d + 64, 5, 64 * (m % 2):64 * (m % 2) + 64]
                    pe.matmul(o, BT[:, c, 64 * h:64 * h + 64], SA_[:, 64 * h4:64 * h4 + 64], start=True, stop=False)
                    mm = pe.matmul(o, KTK[:, c, 64 * h:64 * h + 64], VT[:, c, 64 * h:64 * h + 64], start=False, stop=True)
                if c < TC - 1:
                    mm.then_inc(sem("s_up"), 1)
                for h4, m, d in heads:
                    s, h, o = slice(64 * d, 64 * d + 64), 2 * m + d, PS[:, 2 + d, 64 * (m % 2):64 * (m % 2) + 64]
                    pe.matmul(o, SCO[h4][:, 1, block_of(c)], SA_[:, 64 * h4:64 * h4 + 64], start=True, stop=False)
                    mm = pe.matmul(o, SCO[h4][:, 3, block_of(c)], VT[:, c, 64 * h:64 * h + 64], start=False, stop=(c == 0))
                    if c:
                        mm = pe.matmul(o, AR[m][s, c, 1, :], HS_[s, m % 2, :], start=False, stop=True)
                mm.then_inc(sem("s_out"), 1)

        def state_act(act, hf):
            for c in range(TC):
                k = TC * hf + c
                act.wait_ge(*count("s_rhs", k + 1))
                act.activation(grid(SP_.rearrange("p a b -> p (a b)"), 2), PS[:, 0:2, 0:P], ACT.Copy).then_inc(sem("s_rhs_copied"), 1)
                act.wait_ge(*count("s_sa", k + 1))
                if k:
                    act.wait_ge(*count("s_out", k))
                act.activation(SA_, PS[:, 4, 0:256], ACT.Copy, scale=-1.0).then_inc(sem("s_sa_copied"), 1)

        def state_dve(dve, hf):
            def col(t, c):
                return spread(t[:, 2 * hf:2 * hf + 2, c], 64)

            for c in range(TC):
                k = TC * hf + c
                if c < TC - 1:
                    u = 3 * hf + c
                    dve.wait_ge(*count("s_up", u + 1))
                    up = grid(PS[:, 5, 0:P], 2)
                    dst = HH_ if c == 0 else HT_
                    if u:
                        dve.wait_ge(*count("s_state", u))
                        dve.wait_ge(*count("s_scaled", u))
                    dve.tensor_tensor(dst, up, col(e_rest, c), ALU.mult).then_inc(sem("s_grown"), 1)
                    dve.wait_ge(*count("s_grown", u + 1))
                    if c == 0:
                        dve.tensor_copy(HT_, HH_).then_inc(sem("s_state"), 1)
                    else:
                        dve.tensor_tensor(HH_, HH_, col(e_end, c), ALU.mult).then_inc(sem("s_faded"), 1)
                        dve.wait_ge(*count("s_faded", 2 * hf + c))
                        dve.tensor_tensor(HH_, HH_, HT_, ALU.add).then_inc(sem("s_state"), 1)
                    dve.wait_ge(*count("s_state", u + 1))
                dve.wait_ge(*count("s_out", k + 1))
                if c < TC - 1:
                    dve.tensor_tensor(HS_, HH_, col(e_mid, c + 1), ALU.mult).then_inc(sem("s_scaled"), 1)
                dve.tensor_copy(YTOK[:, c, 256 * hf:256 * hf + 256].rearrange("p (m d i) -> p m d i", m=2, d=2),
                                PS[:, 2:4, 0:P].rearrange("p d (m i) -> p m d i", m=2)).then_inc(sem("s_y"), 1)

        YSQ = at(B2 + 2048, TC, WA)
        LNR = at(B2 + 15360, 2, WA)
        YBT = at(B2 + 19456, 4, T)
        gm, gv, gl_ = small(32), small(32), small(32)
        s_gneps = small(1)

        def rout_pe(pe):
            pe.wait_ge(*count("s_y", 2 * TC))
            pe.wait_ge(*count("g2_in", 16))
            pe.wait_ge(*count("r_sig", 9))
            for tc in range(TC):
                mm = pe.matmul(PS[:, 4 + tc, :], SIG[:, block_of(tc)], G2, start=True, stop=True)
            mm.then_inc(sem("g_gate"), 1)
            pe.wait_ge(*count("g_yb", 1))
            for m in range(4):
                if m >= 2:
                    pe.wait_ge(*count("g_ybt", m - 1))
                for tc in range(TC):
                    mm = pe.transpose(PS[:, m % 2, block_of(tc)], YTOK[:, tc, block_of(m)], ident)
                mm.then_inc(sem("g_turned"), 1)

        def rout_act(act):
            act.wait_ge(*count("g_cent", 1))
            act.activation(YSQ, YTOK, ACT.Square).then_inc(sem("g_sq"), 1)
            act.wait_ge(*count("g_var", 1))
            act.activation(gl_, gv, ACT.Ln, bias=s_gneps, scale=1.0 / 64).then_inc(sem("g_ln"), 1)
            act.wait_ge(*count("g_ln", 1))
            act.activation(gv, gl_, ACT.Exp, scale=-0.5).then_inc(sem("g_ln"), 1)
            for m in range(4):
                act.wait_ge(*count("g_turned", m + 1))
                act.activation(YBT[:, m, :], PS[:, m % 2, :], ACT.Copy).then_inc(sem("g_ybt"), 1)

        def rout_dve(dve):
            Y32 = YTOK.rearrange("p t (h i) -> p (t h) i", h=H2)
            Yf = YTOK.rearrange("p t n -> p (t n)")
            Q32 = YSQ.rearrange("p t (h i) -> p (t h) i", h=H2)
            dve.memset(s_gneps, GN_EPS).then_inc(sem("g_step"), 1)
            dve.wait_ge(*count("s_y", 2 * TC))
            dve.tensor_reduce(gm, Y32, AX.X, ALU.add).then_inc(sem("g_step"), 1)
            dve.wait_ge(*count("g_step", 2))
            dve.tensor_scalar(gm, gm, 1.0 / 64, None, ALU.mult).then_inc(sem("g_step"), 1)
            dve.wait_ge(*count("g_step", 3))
            dve.tensor_tensor(Y32, Y32, spread(gm, 64), ALU.subtract).then_inc(sem("g_cent"), 1)
            dve.wait_ge(*count("g_sq", 1))
            dve.tensor_reduce(gv, Q32, AX.X, ALU.add).then_inc(sem("g_var"), 1)
            dve.wait_ge(*count("g_ln", 2))
            dve.wait_ge(*count("g_cent", 1))
            dve.tensor_tensor(Y32, Y32, spread(gv, 64), ALU.mult).then_inc(sem("g_step"), 1)
            dve.wait_ge(*count("ln_in", 16))
            dve.wait_ge(*count("g_step", 4))
            dve.tensor_tensor(YTOK, YTOK, every(LNR[:, 0, :], TC), ALU.mult).then_inc(sem("g_step"), 1)
            dve.wait_ge(*count("g_var", 1))
            dve.tensor_tensor(Q32, VT.rearrange("p t (h i) -> p (t h) i", h=H2),
                              spread(bon.rearrange("p t h -> p (t h)"), 64), ALU.mult).then_inc(sem("g_step"), 1)
            dve.wait_ge(*count("g_step", 6))
            dve.tensor_tensor(YTOK, YTOK, every(LNR[:, 1, :], TC), ALU.add).then_inc(sem("g_step"), 1)
            dve.wait_ge(*count("g_step", 7))
            dve.tensor_tensor(YTOK, YTOK, YSQ, ALU.add).then_inc(sem("g_step"), 1)
            dve.wait_ge(*count("g_step", 8))
            dve.wait_ge(*count("g_gate", 1))
            dve.tensor_tensor(YTOK, YTOK, PS[:, 4:8, :], ALU.mult).then_inc(sem("g_yb"), 1)

        UT = at(B2 + 15360, TC, D)
        ROWM = at(B2 + 25600, D)

        def merge2_pe(pe):
            pe.wait_ge(*count("g_yb", 1))
            pe.wait_ge(*count("g_ybt", 4))
            for k in range(4):
                for m in range(4):
                    (await2 if m < 2 else await_split2)(pe, ("m", k, m))
                    if m == 2 and k == 0:
                        pe.wait_ge(*count("low2_back", 32))
                    if k:
                        pe.wait_ge(*count("m2_done", 4 * (k - 1) + (2, 4, 2, 4)[m]))
                    for j in range(2):
                        out = PS[:, 2 * m + j, :]
                        if m < 2:
                            w, src = slot2(("m", k, m)), (YAT, YBT)[m]
                            for dc in range(4):
                                mm = pe.matmul(out, w[:, dc, P * j:P * j + P], src[:, dc, :],
                                               start=(dc == 0), stop=(dc == 3))
                        else:
                            mm = split_tile(pe, out, parts2(("m", k, m)), P * j, LOW3G)
                        mm.then_inc(sem("m2_proj"), 1)
            pe.wait_ge(*count("m2_sum", DC))
            pe.wait_ge(*count("m2_done", 16))
            for p in range(16):
                j, tc = p // 4, p % 4
                if tc == 0:
                    await2(pe, ("o", j))
                if p >= 8:
                    pe.wait_ge(*count("o2_copied", p - 7))
                token_tile(pe, PS[:, p % 8, 0:256], slot2(("o", j)), MT, tc).then_inc(sem("o2_proj"), 1)

        def merge2_act(act):
            for k in range(4):
                for m in (2, 3):
                    split2_act(act, ("m", k, m))
                for m in (2, 3):
                    for j in range(2):
                        act.wait_ge(*count("m2_proj", 8 * k + 2 * m + j + 1))
                        if k:
                            act.wait_ge(*count("m2_done", 4 * (k - 1) + 2 * (m - 2) + j + 1))
                        g = 8 * (m - 2) + 2 * k + j
                        act.activation(MG_T[:, 2 * (m - 2) + j, :], PS[:, 2 * m + j, :], ACT.Tanh, scale=0.5,
                                       bias=s_gbh[:, g:g + 1]).then_inc(sem("m2_tanh"), 1)
            for p in range(16):
                j, tc = p // 4, p % 4
                act.wait_ge(*count("o2_proj", p + 1))
                act.activation(UT[:, tc, 256 * j:256 * j + 256], PS[:, p % 8, 0:256], ACT.Copy, scale=0.5)\
                    .then_inc(sem("o2_copied"), 1)
            post_norm_act(act, "pn1", [("o2_copied", 16)], UT)

        def merge2_dve(dve):
            for k in range(4):
                for m in range(2):
                    for j in range(2):
                        dve.wait_ge(*count("m2_tanh", 4 * k + 2 * m + j + 1))
                        dst = MT[:, 2 * k + j, :] if m == 0 else MG_N[:, j, :]
                        if m and k:
                            dve.wait_ge(*count("m2_sum", 2 * k - 1 + j))
                        dve.scalar_tensor_tensor(dst, MG_T[:, 2 * m + j, :], 1.0, PS[:, 2 * m + j, :], ALU.add, ALU.mult)\
                            .then_inc(sem("m2_done"), 1)
                for j in range(2):
                    dve.wait_ge(*count("m2_done", 4 * k + 3 + j))
                    dve.tensor_tensor(MT[:, 2 * k + j, :], MT[:, 2 * k + j, :], MG_N[:, j, :], ALU.add)\
                        .then_inc(sem("m2_sum"), 1)
            dve.wait_ge(*count("x2_back", 32))
            post_norm_dve(dve, "pn1", UT, ROWM)

        SQJ = at(B2 + 24576, D)

        def post_norm_act(act, tag, ready, U):
            for s, v in ready:
                act.wait_ge(*count(s, v))
            for tc in range(TC):
                if tc:
                    act.wait_ge(*count(tag + "_sq", tc))
                act.activation(SQJ, U[:, tc, :], ACT.Square, accum_out=ss[:, tc:tc + 1]).then_inc(sem(tag + "_sq"), 1)
            act.wait_ge(*count(tag + "_sq", TC))
            act.activation(lnv, ss, ACT.Ln, bias=eps, scale=1.0 / D).then_inc(sem(tag + "_ln"), 1)
            act.wait_ge(*count(tag + "_ln", 1))
            act.activation(rs, lnv, ACT.Exp, scale=-0.5).then_inc(sem(tag + "_r"), 1)

        def post_norm_dve(dve, tag, U, ROW):
            dve.wait_ge(*count(tag + "_r", 1))
            for tc in range(TC + 1):
                if tc < TC:
                    dve.scalar_tensor_tensor(U[:, tc, :], U[:, tc, :], rs[:, tc:tc + 1], ROW, ALU.mult, ALU.mult)\
                        .then_inc(sem(tag + "_u"), 1)
                if tc:
                    dve.wait_ge(*count(tag + "_u", tc))
                    dve.tensor_tensor(X[:, tc - 1, :], X[:, tc - 1, :], U[:, tc - 1, :], ALU.add)\
                        .then_inc(sem(tag + "_x"), 1)

        U1 = at(B2, D_FF // P, T)
        RL = at(B2 + 25600, 2, T)
        UD = at(B2 + 16384, TC, D)
        ROWF = at(B2 + 20480, D)

        def ffn_pe(pe):
            pe.wait_ge(*count("pn1_x", TC))
            norm_pe(pe, "n4")
            pe.wait_ge(*count("n4_lo", DC))
            for t in range(D_FF // P):
                if t % 2 == 0:
                    await_split2(pe, ("u", t // 2))
                if t >= 2:
                    pe.wait_ge(*count("up_relu", t - 1))
                split_tile(pe, PS[:, t % 2, :], parts2(("u", t // 2)), P * (t % 2), LOW4).then_inc(sem("up_proj"), 1)
            pe.wait_ge(*count("up_relu", D_FF // P))
            for f in range(D_FF // P):
                if f % 2 == 0:
                    await2(pe, ("d", f // 2))
                pe.wait_ge(*count("up_sq", f + 1))
                w = slot2(("d", f // 2))
                for n in range(8):
                    tc, half = n // 2, n % 2
                    mm = pe.matmul(PS[:, n, :], U1[:, f, block_of(tc)], w[:, f % 2, 512 * half:512 * half + 512],
                                   start=(f == 0), stop=(f == D_FF // P - 1))
                if f % 2 == 1:
                    mm.then_inc(sem("dn_proj"), 1)

        def ffn_act(act):
            split2_act(act, ("u", 0))
            norm_act(act, "n4", [("pn1_x", TC)], "pre_ffn")
            for t in range(D_FF // P):
                if t % 2 == 0 and t < D_FF // P - 2:
                    split2_act(act, ("u", t // 2 + 1))
                act.wait_ge(*count("up_proj", t + 1))
                if t >= 2:
                    act.wait_ge(*count("up_sq", t - 1))
                act.activation(RL[:, t % 2, :], PS[:, t % 2, :], ACT.Relu).then_inc(sem("up_relu"), 1)
            act.wait_ge(*count("dn_proj", 16))
            for n in range(8):
                act.activation(UD[:, n // 2, 512 * (n % 2):512 * (n % 2) + 512], PS[:, n, :], ACT.Copy)\
                    .then_inc(sem("dn_copied"), 1)
            post_norm_act(act, "pn2", [("dn_copied", 8)], UD)

        def ffn_dve(dve):
            norm_dve(dve, "n4")
            norm_low_dve(dve, "n4", LOW4, "pre_ffn")
            for t in range(D_FF // P):
                dve.wait_ge(*count("up_relu", t + 1))
                dve.tensor_tensor(U1[:, t, :], RL[:, t % 2, :], RL[:, t % 2, :], ALU.mult).then_inc(sem("up_sq"), 1)
            dve.wait_ge(*count("rowf_in", 16))
            post_norm_dve(dve, "pn2", UD, ROWF)

        def block2_pe(pe):
            pe.wait_ge(*count("x2_done", TC))
            bias_pe(pe)
            norm_pe(pe, "n3")
            band_pe(pe)
            shift_pe(pe)
            tiles_pe(pe)
            for hf in range(2):
                units_pe(pe, 2 * hf)
                units_pe(pe, 2 * hf + 1)
                state_pe(pe, hf)
            rout_pe(pe)
            merge2_pe(pe)
            ffn_pe(pe)

        def block2_act(act):
            norm_act(act, "n3", [("x2_done", TC)], "pre_mix")
            split2_act(act, ("qk", 0))
            band_act(act)
            shift_act(act)
            tiles_act(act)
            for hf in range(2):
                for m in (2 * hf, 2 * hf + 1):
                    inverse_act(act, GH + m, lanes2(m))
                state_act(act, hf)
            rout_act(act)
            merge2_act(act)
            ffn_act(act)

        def block2_dve(dve):
            norm_dve(dve, "n3")
            bias_tiles_dve(dve)
            norm_low_dve(dve, "n3", LOW3, "pre_mix")
            band_dve(dve)
            shift_dve(dve)
            tiles_dve(dve)
            for hf in range(2):
                units_dve(dve, 2 * hf)
                units_dve(dve, 2 * hf + 1)
                state_dve(dve, hf)
            rout_dve(dve)
            merge2_dve(dve)
            ffn_dve(dve)

        def block2_pool(pool):
            splits2_pool(pool, ("qk", "v", "r"))
            for m in range(4):
                units_pool(pool, m)
            pool.wait_ge(*count("low2_out", 32))
            pool.wait_ge(*count("s_y", 2 * TC))
            pool.wait_ge(*count("g_gate", 1))
            for s in range(2):
                pool.dma_start(r32(half_at(B2 + 24576, s)), low2_dram[:, s * SLOT:(s + 1) * SLOT])\
                    .then_inc(sem("low2_back"), 16)
            splits2_pool(pool, ("m", "u"))

        def block2_sp(sp):
            sp.wait_ge(*count("mo_used", 24 * PAIRS))
            last_scatter = ("mo_scattered", 8 * PAIRS)
            for n, (src, shape, done, value) in enumerate(loads2):
                if n == 0:
                    sp.wait_ge(*count(last_scatter[0], last_scatter[1]))
                if n == 0:
                    rows_on = bass.AP(toe_dram.tensor, 0, [[1, P], [TOE, H2], [1, T]])
                    sp.wait_ge(*count("ext_out", 16))
                    sp.dma_start(TBR, rows_on).then_inc(sem("toe_in"), 16)
                if n == where2[("r", 0)]:
                    sp.wait_ge(*count("n3_lo", DC))
                    sp.dma_start(x2_dram, S[:, M_X:M_X + TC * D]).then_inc(sem("x2_kept"), 16)
                    for s in range(2):
                        sp.dma_start(low2_dram[:, s * SLOT:(s + 1) * SLOT], rounded(half_at(B2 + 22528, s)))\
                            .then_inc(sem("low2_out"), 16)
                if n == where2[("r", 6)]:
                    sp.wait_ge(*count("b_yat", 4))
                    sp.dma_start(W2[0:64, :], a["w2_2"][0]).then_inc(sem("lora_in"), 16)
                    sp.dma_start(A2[64:128, :], a["a2_2"][0]).then_inc(sem("lora_in"), 16)
                    sp.dma_start(G2, a["g2_2"][0]).then_inc(sem("g2_in"), 16)
                if n == where2[("m", 0, 0)]:
                    sp.wait_ge(*count("s_y", 2 * TC))
                    sp.dma_start(LNR.rearrange("p a b -> p (a b)"), a["rows"][3].unsqueeze(0).to_broadcast([P, D]))\
                        .then_inc(sem("ln_in"), 16)
                if n == where2[("o", 1)]:
                    sp.wait_ge(*count("m2_proj", 32))
                    sp.dma_start(S[:, M_X:M_X + TC * D], x2_dram).then_inc(sem("x2_back"), 16)
                    sp.dma_start(ROWM, a["rows"][1].unsqueeze(0).to_broadcast([P, D])).then_inc(sem("x2_back"), 16)
                if n == where2[("d", 0)]:
                    sp.wait_ge(*count("pn1_x", TC))
                    sp.dma_start(ROWF, a["rows"][2].unsqueeze(0).to_broadcast([P, D])).then_inc(sem("rowf_in"), 16)
                if n >= SLOTS:
                    sp.wait_ge(*count(loads2[n - SLOTS][2], loads2[n - SLOTS][3]))
                sp.dma_start(slot2(list(where2)[n]), src).then_inc(sem(f"w2_loaded{n % SLOTS}"), 16)
            out_v = a["out"][0].rearrange("(tc p) d -> p tc d", p=P)
            for tc in range(TC):
                sp.wait_ge(*count("pn2_x", tc + 1))
                sp.dma_start(out_v[:, tc, :], X[:, tc, :]).then_inc(sem("stored"), 16)
            sp.wait_ge(*count("stored", 16 * TC))

        block = ctx.enter_context(nc.Block())

        @block.sync
        def _(sp):
            sp.dma_start(X, a["x"][0].rearrange("(tc p) d -> p tc d", p=P)).then_inc(sem("x_in"), 16)
            sp.dma_start(S[:, M_VEC:M_VEC + VEC_W], a["vectors"]).then_inc(sem("small_in"), 16)
            lv = a["lam"]
            sp.dma_start(row("lam"), lv.unsqueeze(0).to_broadcast([P, 256])).then_inc(sem("small_in"), 16)
            sp.dma_start(S[:, M_ROWS:M_ROWS + 32], a["dt_a"].unsqueeze(0).to_broadcast([P, 32])).then_inc(sem("small_in"), 16)
            sp.dma_start(S[:, M_CONST:M_CONST + CONST_W], a["shape_constants"]).then_inc(sem("const_in"), 16)
            sp.dma_start(wab, a["w_in"][0, :, C_AB:C_AB + 32].rearrange("(dc p) n -> p dc n", p=P))\
                .then_inc(sem("wab_in"), 16)
            sp.dma_start(REV[0:H2, :], a["rel_reversed"]).then_inc(sem("rev_in"), 16)
            for n, (src, done, value) in enumerate(loads):
                if n == where[("v", 0)]:
                    sp.wait_ge(*count("ext_set", 3))
                    sp.dma_start(toe_dram, EXT[0:H2, :]).then_inc(sem("ext_out"), 16)
                    sp.wait_ge(*count("n1_lo", DC))
                    for s in range(2):
                        sp.dma_start(htl_dram[:, s * SLOT:(s + 1) * SLOT], rounded(half_at(M_DYN + 16384, s)))\
                            .then_inc(sem("low_out"), 16)
                if n == where[("g", 0, 0)]:
                    sp.wait_ge(*count("an_ot", AH))
                    sp.dma_start(ot_dram, S[:, M_DYN:M_DYN + 8 * T]).then_inc(sem("ot_out"), 16)
                if n in (where[("g", 1, 2)], where[("z", 2)]):
                    for d in range(2):
                        sp.wait_ge(*count(f"sc_o{d}", TC * (1 if n == where[("g", 1, 2)] else 2)))
                if n == where[("m", 0, 0)]:
                    sp.wait_ge(*count("ot_out", 16))
                    sp.dma_start(S[:, M_DYN:M_DYN + 8 * T], ot_dram).then_inc(sem("ot_back"), 16)
                if n >= SLOTS:
                    sp.wait_ge(*count(loads[n - SLOTS][1], loads[n - SLOTS][2]))
                sp.dma_start(slot_of(list(where)[n]), src).then_inc(sem(f"w_loaded{n % SLOTS}"), 16)
                if n == where[("o", 0)]:
                    sp.wait_ge(*count("mg_proj", 28))
                    sp.dma_start(X, a["x"][0].rearrange("(tc p) d -> p tc d", p=P)).then_inc(sem("x_back"), 16)
            moe_sp(sp)
            block2_sp(sp)

        @block.tensor
        def _(pe):
            norm_pe(pe, "n1")
            attention_pe(pe)
            GDN_PE(pe)
            router_pe(pe)
            experts_pe(pe)
            block2_pe(pe)

        @block.scalar
        def _(act):
            act.wait_ge(*count("eps_set", 1))
            act.wait_ge(*count("small_in", 48))
            norm_act(act, "n1", [("x_in", 16)], "norm1")
            split_act(act, ("qk", 0))
            attention_act(act)
            GDN_ACT(act)
            router_act(act)
            experts_act(act)
            final1_act(act)
            block2_act(act)

        @block.vector
        def _(dve):
            prepare_dve(dve)
            dve.wait_ge(*count("const_in", 16))
            norm_dve(dve, "n1")
            norm_low_dve(dve, "n1", HTL, "norm1")
            bias_dve(dve)
            attention_dve(dve)
            GDN_DVE(dve)
            router_dve(dve)
            experts_dve(dve)
            final1_dve(dve)
            block2_dve(dve)

        @block.gpsimd
        def _(pool):
            attention_pool(pool)
            GDN_POOL(pool)
            gate_pool(pool)
            block2_pool(pool)


def host_layout(inputs):
    f = {n: np.ascontiguousarray(v) for n, v in inputs.items()}
    out = {n: f[n] for n in ("x", "w_in", "w_proj_attn", "w_proj_gdn", "w_out", "w_router", "w_gate", "w_up", "w_down",
                             "w_in_2", "w2_2", "a2_2", "g2_2", "proj_a_2", "proj_b_2", "w_out_2", "w_up_2", "w_down_2")}

    def columns(v):
        return np.ascontiguousarray(v.reshape(-1, P).T)

    parts = {
        "norm1": columns(f["norm1_w"]), "norm2": columns(f["norm2_w"]), "subln": columns(f["subln_w"]),
        "gdn_norm": columns(f["gdn_norm_w"]),
        "conv": f["conv_w"][0].reshape(5, 24, P).transpose(2, 1, 0).reshape(P, 120),
        "pre_mix": columns(f["pre_mix_g_2"]), "pre_ffn": columns(f["pre_ffn_g_2"]),
        "gate_bias": columns(f["gate_bias_2"]), "mu": columns(f["shift_mu_2"]), "w0": columns(f["w0_2"]),
        "a0": columns(f["a0_2"]), "k_k": columns(f["k_k_2"]), "k_a": columns(f["k_a_2"]), "r_k": columns(f["r_k_2"]),
    }
    out["vectors"] = np.ascontiguousarray(np.concatenate([parts[n] for n in VEC], axis=1))
    out["lam"] = np.concatenate([f[n][0] for n in ("lambda_q1", "lambda_k1", "lambda_q2", "lambda_k2")])
    out["dt_a"] = np.concatenate([f[n][0] for n in ("dt_bias_fwd", "dt_bias_bwd", "a_log_fwd", "a_log_bwd")])
    out["rows"] = np.ascontiguousarray(np.stack([f["norm_f_w"], f["post_mix_g_2"][0], f["post_ffn_g_2"][0],
                  np.concatenate([f["ln_x_w_2"][0], f["ln_x_b_2"][0]])]))
    out["rel_reversed"] = np.ascontiguousarray(f["rel_bias_2"][0][:, ::-1])
    out["shape_constants"] = shape_constants()
    return out


def kernel(**inputs):
    import concourse.bacc as bacc
    from concourse.bass_utils import run_bass_kernel_spmd
    arrays = host_layout({n: np.asarray(v) for n, v in inputs.items()})
    nc = bacc.Bacc("TRN2", target_bir_lowering=False, num_devices=1)
    a = {n: nc.dram_tensor("in_" + n, v.shape, mybir.dt.from_np(v.dtype), kind="ExternalInput").ap()
         for n, v in arrays.items()}
    a["out"] = nc.dram_tensor("out", (1, T, D), F32, kind="ExternalOutput").ap()
    build_program(nc, a)
    nc.compile()
    res = run_bass_kernel_spmd(nc, [{"in_" + n: v for n, v in arrays.items()}], core_ids=[0])
    return np.asarray(res.results[0]["out"], dtype=np.float32)
```
